# Optimizing a Trainium2 kernel written in Bass

```python
import jax, jax.numpy as jnp
from jax import lax
import numpy as np

D_MODEL = 1024
BATCH = 1
SEQ = 512
DEPTH = 1
DEC_BATCH = 1
DEC_SEQ = 32
PAST_LEN = 128

CHUNK = 64
WINDOW = 128
WIN_CHUNKS = WINDOW // CHUNK
BAND = (WIN_CHUNKS + 1) * CHUNK
D_MIX = D_MODEL
HEAD_DIM = 64
N_HEADS = 8
N_KV_HEADS = 2
GQA_GROUP = N_HEADS // N_KV_HEADS
D_ATTN = N_HEADS * HEAD_DIM
D_KV = N_KV_HEADS * HEAD_DIM
D_CONV = D_MIX - D_ATTN
CONV_WIDTH = 3
D_FF = 2816
D_PLE = 256
RMS_EPS = 1e-6
ATTN_SCALE = HEAD_DIM ** -0.5
Q_END = D_ATTN
K_END = Q_END + D_KV
V_END = K_END + D_KV
B_END = V_END + D_CONV
C_END = B_END + D_CONV
D_IN = C_END + D_CONV

kernel_name = 'hymba_swa_sink_shortconv_macaron_ple_step'

def rms_norm(x, g):
    x32 = x.astype(jnp.float32)
    y = x32 * lax.rsqrt(jnp.mean(x32 * x32, axis=-1, keepdims=True) + RMS_EPS)
    return (y * g.astype(jnp.float32)).astype(x.dtype)

def swiglu_ffn(x, w_gate_up, w_down):
    g, u = jnp.split(x @ w_gate_up, 2, axis=-1)
    return (jax.nn.silu(g) * u) @ w_down

def sink_softmax(scores, sinks):
    s = sinks.astype(jnp.float32).reshape(N_KV_HEADS, GQA_GROUP)[:, :, None, None]
    m = jnp.maximum(jnp.max(scores, axis=-1, keepdims=True), s)
    e = jnp.exp(scores - m)
    return e / (jnp.sum(e, axis=-1, keepdims=True) + jnp.exp(s - m))

def window_attention_prompt(q, k, v, sinks):
    b, s = q.shape[:2]
    n_c = s // CHUNK
    qc = q.reshape(b, n_c, CHUNK, N_KV_HEADS, GQA_GROUP, HEAD_DIM)

    def band(t):
        tc = t.reshape(b, n_c, CHUNK, N_KV_HEADS, HEAD_DIM)
        tp = jnp.pad(tc, ((0, 0), (WIN_CHUNKS, 0), (0, 0), (0, 0), (0, 0)))
        return jnp.concatenate([tp[:, j:j + n_c] for j in range(WIN_CHUNKS + 1)], axis=2)

    kb, vb = band(k), band(v)
    key_chunk = jnp.arange(n_c)[:, None] - WIN_CHUNKS + (jnp.arange(BAND) // CHUNK)[None, :]
    valid = (key_chunk >= 0)[None, :, None, None, None, :]
    scores = jnp.einsum('bcqkgd,bcskd->bckgqs', qc, kb, preferred_element_type=jnp.float32) * ATTN_SCALE
    scores = jnp.where(valid, scores, -jnp.inf)
    probs = sink_softmax(scores, sinks).astype(vb.dtype)
    out = jnp.einsum('bckgqs,bcskd->bcqkgd', probs, vb)
    return out.reshape(b, s, D_ATTN), k[:, -WINDOW:], v[:, -WINDOW:]

def window_attention_sample(q, k, v, sinks, k_cache, v_cache):
    b, t = q.shape[:2]
    qg = q.reshape(b, t, N_KV_HEADS, GQA_GROUP, HEAD_DIM)
    kk = jnp.concatenate([k_cache.astype(k.dtype), k], axis=1)
    vv = jnp.concatenate([v_cache.astype(v.dtype), v], axis=1)
    scores = jnp.einsum('bqkgd,bskd->bkgqs', qg, kk, preferred_element_type=jnp.float32) * ATTN_SCALE
    probs = sink_softmax(scores, sinks).astype(vv.dtype)
    out = jnp.einsum('bkgqs,bskd->bqkgd', probs, vv)
    return out.reshape(b, t, D_ATTN), kk[:, -WINDOW:], vv[:, -WINDOW:]

def gated_short_conv(b_gate, c_gate, xv, conv_prev, conv_w):
    cin = c_gate * xv
    padded = jnp.concatenate([conv_prev.astype(cin.dtype), cin], axis=1)
    t = cin.shape[1]
    conv = padded[:, 0:t] * conv_w[0]
    for j in range(1, CONV_WIDTH):
        conv = conv + padded[:, j:j + t] * conv_w[j]
    return b_gate * conv, padded[:, -(CONV_WIDTH - 1):]

def encoder_layer(x, p, attend, conv_prev,
                  norm_ffn1_pre, w_ffn1_gate_up, w_ffn1_down, norm_ffn1_post,
                  norm_mix_pre, w_in, conv_w, attn_sinks, norm_attn_out, norm_conv_out, w_out, norm_mix_post,
                  norm_ffn2_pre, w_ffn2_gate_up, w_ffn2_down, norm_ffn2_post,
                  norm_ple_pre, w_ple_gate, w_ple_proj, norm_ple_post):
    r = x + 0.5 * rms_norm(swiglu_ffn(rms_norm(x, norm_ffn1_pre), w_ffn1_gate_up, w_ffn1_down), norm_ffn1_post)
    z = rms_norm(r, norm_mix_pre) @ w_in
    b, t = z.shape[:2]
    q = z[..., :Q_END].reshape(b, t, N_HEADS, HEAD_DIM)
    k = z[..., Q_END:K_END].reshape(b, t, N_KV_HEADS, HEAD_DIM)
    v = z[..., K_END:V_END].reshape(b, t, N_KV_HEADS, HEAD_DIM)
    attn_out, k_state, v_state = attend(q, k, v, attn_sinks)
    conv_out, conv_state = gated_short_conv(z[..., V_END:B_END], z[..., B_END:C_END], z[..., C_END:], conv_prev, conv_w)
    mixed = jnp.concatenate([rms_norm(attn_out, norm_attn_out), rms_norm(conv_out, norm_conv_out)], axis=-1) @ w_out
    r = r + rms_norm(mixed, norm_mix_post)
    r = r + 0.5 * rms_norm(swiglu_ffn(rms_norm(r, norm_ffn2_pre), w_ffn2_gate_up, w_ffn2_down), norm_ffn2_post)
    gate = jax.nn.sigmoid(rms_norm(r, norm_ple_pre) @ w_ple_gate)
    r = r + rms_norm(gate * (p @ w_ple_proj), norm_ple_post)
    return r, k_state, v_state, conv_state

def setup_inputs(seed: int = 0) -> dict:
    key = jax.random.key(seed)
    ks = iter(jax.random.split(key, 40))
    nrm = lambda shape, scale=1.0: jax.random.normal(next(ks), shape, jnp.float32) * scale
    gain = lambda dim: 1.0 + nrm((DEPTH, dim), 0.01)
    return {
        'x_prompt': nrm((BATCH, SEQ, D_MODEL)),
        'x_sample': nrm((DEC_BATCH, DEC_SEQ, D_MODEL)),
        'cache_attn_k': nrm((DEPTH, DEC_BATCH, WINDOW, N_KV_HEADS, HEAD_DIM)),
        'cache_attn_v': nrm((DEPTH, DEC_BATCH, WINDOW, N_KV_HEADS, HEAD_DIM)),
        'cache_conv': nrm((DEPTH, DEC_BATCH, CONV_WIDTH - 1, D_CONV)),
        'p_prompt': nrm((DEPTH, BATCH, SEQ, D_PLE)),
        'p_sample': nrm((DEPTH, DEC_BATCH, DEC_SEQ, D_PLE)),
        'norm_ffn1_pre': gain(D_MODEL),
        'w_ffn1_gate_up': nrm((DEPTH, D_MODEL, 2 * D_FF), D_MODEL ** -0.5),
        'w_ffn1_down': nrm((DEPTH, D_FF, D_MODEL), D_FF ** -0.5),
        'norm_ffn1_post': gain(D_MODEL),
        'norm_mix_pre': gain(D_MODEL),
        'w_in': nrm((DEPTH, D_MODEL, D_IN), D_MODEL ** -0.5),
        'conv_w': nrm((DEPTH, CONV_WIDTH, D_CONV), CONV_WIDTH ** -0.5),
        'attn_sinks': nrm((DEPTH, N_HEADS), 0.5),
        'norm_attn_out': gain(D_ATTN),
        'norm_conv_out': gain(D_CONV),
        'w_out': nrm((DEPTH, D_MIX, D_MODEL), D_MIX ** -0.5),
        'norm_mix_post': gain(D_MODEL),
        'norm_ffn2_pre': gain(D_MODEL),
        'w_ffn2_gate_up': nrm((DEPTH, D_MODEL, 2 * D_FF), D_MODEL ** -0.5),
        'w_ffn2_down': nrm((DEPTH, D_FF, D_MODEL), D_FF ** -0.5),
        'norm_ffn2_post': gain(D_MODEL),
        'norm_ple_pre': gain(D_MODEL),
        'w_ple_gate': nrm((DEPTH, D_MODEL, D_MODEL), D_MODEL ** -0.5),
        'w_ple_proj': nrm((DEPTH, D_PLE, D_MODEL), D_PLE ** -0.5),
        'norm_ple_post': gain(D_MODEL),
    }

def reference(x_prompt, x_sample, cache_attn_k, cache_attn_v, cache_conv, p_prompt, p_sample,
              norm_ffn1_pre, w_ffn1_gate_up, w_ffn1_down, norm_ffn1_post,
              norm_mix_pre, w_in, conv_w, attn_sinks, norm_attn_out, norm_conv_out, w_out, norm_mix_post,
              norm_ffn2_pre, w_ffn2_gate_up, w_ffn2_down, norm_ffn2_post,
              norm_ple_pre, w_ple_gate, w_ple_proj, norm_ple_post):
    hp, hs = x_prompt, x_sample
    kp_list, vp_list, cp_list, ksm_list, vsm_list, csm_list = [], [], [], [], [], []
    for i in range(DEPTH):
        w = (norm_ffn1_pre[i], w_ffn1_gate_up[i], w_ffn1_down[i], norm_ffn1_post[i],
             norm_mix_pre[i], w_in[i], conv_w[i], attn_sinks[i], norm_attn_out[i], norm_conv_out[i], w_out[i],
             norm_mix_post[i], norm_ffn2_pre[i], w_ffn2_gate_up[i], w_ffn2_down[i], norm_ffn2_post[i],
             norm_ple_pre[i], w_ple_gate[i], w_ple_proj[i], norm_ple_post[i])
        conv_zero = jnp.zeros((hp.shape[0], CONV_WIDTH - 1, D_CONV), hp.dtype)
        hp, kp, vp, cp = encoder_layer(hp, p_prompt[i], window_attention_prompt, conv_zero, *w)
        attend_sample = lambda q, k, v, s, ck=cache_attn_k[i], cv=cache_attn_v[i]: window_attention_sample(q, k, v, s, ck, cv)
        hs, ksm, vsm, csm = encoder_layer(hs, p_sample[i], attend_sample, cache_conv[i], *w)
        kp_list.append(kp); vp_list.append(vp); cp_list.append(cp)
        ksm_list.append(ksm); vsm_list.append(vsm); csm_list.append(csm)
    new_k_prompt = jnp.stack(kp_list)
    new_v_prompt = jnp.stack(vp_list)
    new_conv_prompt = jnp.stack(cp_list)
    new_k_sample = jnp.stack(ksm_list)
    new_v_sample = jnp.stack(vsm_list)
    new_conv_sample = jnp.stack(csm_list)
    return (hp, hs, new_k_prompt, new_v_prompt, new_conv_prompt, new_k_sample, new_v_sample, new_conv_sample)


_drawn_inputs = setup_inputs


def setup_inputs(seed=0):
    import zlib

    import numpy as np

    out = dict(_drawn_inputs(seed))
    spreads = {}
    factors = {'norm_ffn1_pre': 5.996,
     'norm_ffn1_post': 8.0,
     'norm_mix_pre': 3.765,
     'attn_sinks': 64.0,
     'norm_attn_out': 198.06,
     'norm_conv_out': 198.196,
     'norm_mix_post': 46.658,
     'norm_ffn2_pre': 197.291,
     'norm_ffn2_post': 200.0,
     'norm_ple_pre': 171.639,
     'norm_ple_post': 200.0,
     'cache_conv': 4.669}
    for name, (base, spread) in spreads.items():
        noise = np.random.default_rng([zlib.crc32(name.encode()), seed]).standard_normal(out[name].shape)
        drawn = base * np.exp(spread * noise) if base else spread * noise
        out[name] = __import__('jax').numpy.asarray(drawn.astype(out[name].dtype))
    for name, factor in factors.items():
        out[name] = (out[name] * factor).astype(out[name].dtype)
    return out
```

```python
from contextlib import ExitStack

import concourse.bass as bass
from concourse import mybir

F32 = mybir.dt.float32
F32R = mybir.dt.float32r
ALU = mybir.AluOpType
ACT = mybir.ActivationFunctionType
AX_X = mybir.AxisListType.X

P = 128
SLOTS = 4
MAXK = 11
A, B = 0, 1


def encoder_layer(nc, t):
    SEQ, D = t["x_prompt"].shape[1:]
    DEC = t["x_sample"].shape[1]
    T = SEQ + DEC
    HT = T // 2
    KD = D // P
    FF = t["w_ffn1_down"].shape[1]
    KF = FF // P
    WINDOW = t["cache_attn_k"].shape[2]
    KP = t["p_prompt"].shape[3] // P
    DA = t["norm_attn_out"].shape[1]
    KA = DA // P
    CHUNK, DH = 64, 64
    SCALE = DH ** -0.5
    EPS = 1e-6
    NCH = SEQ // CHUNK
    TB = SEQ - HT
    XT = SEQ // P + 1
    VE = DA + 2 * P
    assert KF == 2 * MAXK and KD + KP <= MAXK and WINDOW == P and D == 2 * DA and KD == 8 and KA == 4

    MIX = ["k", "v", "q0", "q1", "q2", "q3", "c0", "x0", "c1", "x1", "b0", "b1",
           "c2", "x2", "c3", "x3", "b2", "b3"]
    STAGES = [("up1", 2 * KF, 4 * KF, KD), ("down1", 2 * KD, 2 * KD, MAXK), ("mix", len(MIX), 2 * len(MIX), KD),
              ("out", KD, 2 * KD, KD), ("up2", 2 * KF, 4 * KF, KD), ("down2", 2 * KD, 2 * KD, MAXK),
              ("ple", KD, 4 * KD, KD + KP)]
    C0, U0, stage_of, width_of, loads_of = {}, {}, [], [], []
    chunks = units = 0
    for name, n, un, kt in STAGES:
        C0[name], U0[name] = chunks, units
        chunks, units = chunks + n, units + un
        stage_of += [name] * n
        width_of += [kt] * n
        loads_of += [{"out": 3, "ple": 2}.get(name, 2 if name == "mix" and MIX[j][0] == "q" else 1)
                     for j in range(n)]
    NCHUNK = chunks
    UP_GROUPS, DOWN_GROUPS = KF // 2, KD // 2

    def loaded_value(c):
        return 16 * sum(loads_of[c % SLOTS:c + 1:SLOTS])

    COL, nrows = {}, 0
    for name, n in (("norm_ffn1_pre", KD), ("norm_ffn1_post", KD), ("norm_mix_pre", KD),
                    ("norm_attn_out", KA), ("norm_conv_out", KA), ("conv_w", 3 * KA),
                    ("norm_mix_post", KD), ("norm_ffn2_pre", KD), ("norm_ffn2_post", KD),
                    ("norm_ple_pre", KD), ("norm_ple_post", KD), ("cache_conv", 2 * KA)):
        COL[name] = nrows
        nrows += n

    CHAIN = [(None, "norm_ffn1_pre"), ("norm_ffn1_post", "norm_mix_pre"), ("norm_mix_post", "norm_ffn2_pre"),
             ("norm_ffn2_post", "norm_ple_pre"), ("norm_ple_post", None)]
    SQ0 = {"start": 0, "down1": 16, "mix": 48, "out": 64, "down2": 96, "ple": 128}
    Y0 = {"down1": 0, "out": 2 * KD, "down2": 4 * KD}
    PAIR0 = {"up1": 0, "up2": 2 * KF, "ple": 4 * KF}
    HALF0 = {"down1": 0, "down2": KD}
    SUM0 = {"start": 0, "down1": 2, "mix": 6, "out": 10, "down2": 14, "ple": 18}
    SUMMED = [8, 16, 30, 38, 40, 48, 52, 56, 60, 64, 76, 84, 88, 96, 110, 118, 120, 128, 140, 144]
    PLE_UNITS = [(i, h) for g in (0, 2) for h in (A, B) for i in (g, g + 1)]

    TASKS = [(c, p) for c in range(NCH) for p in range(2)] + [("sample", 0)]
    NTASK = len(TASKS)
    MIX_ATTN0 = 16

    ctx = ExitStack()
    with ctx:
        def sb(name, shape, dt=F32):
            return ctx.enter_context(nc.sbuf_tensor(name, shape, dt))

        def sem(name):
            return ctx.enter_context(nc.semaphore(name))

        def overlay(shapes):
            with ExitStack() as o:
                return [o.enter_context(nc.sbuf_tensor(n, s, d)) for n, s, d in shapes]

        r = sb("r", [P, KD, T])
        x_hi = sb("x_hi", [P, KD, T], F32R)
        y_down, = overlay([("y_down", [P, KD, T], F32)])
        x_lo = sb("x_lo", [P, KD, T], F32R)
        raw = sb("raw", [P, SLOTS, MAXK, P])
        w_hi = sb("w_hi", [P, SLOTS, MAXK, P], F32R)
        w_lo = sb("w_lo", [P, SLOTS, MAXK, P], F32R)
        rpre = sb("rpre", [P, 2, HT])
        ssq = sb("ssq", [P, 2, HT])
        sq = sb("sq", [P, 2, HT])
        tG = sb("tG", [P, 2, HT])
        tU = sb("tU", [P, 2, HT])
        ident = sb("ident", [P, P])
        ones = sb("ones", [P, P])
        gT = sb("gT", [P, nrows])
        eps = sb("eps", [P, 1])
        x_tok, g_rows = overlay([("x_tok", [P, XT, D], F32), ("g_rows", [nrows, P], F32)])
        (m_hi, ac, zq, cv, cinp, zk, zv, v_band, probs, probs_t, k_cache, v_cache, k_new, k_own, v_own,
         conv_rows, conv_new, rmix, ssm, sinks, sink, nsink, mx, nm, se, es, rs, den) = overlay([
             ("m_hi", [P, KD, T], F32R),
             ("ac", [P, KD, T], F32),
             ("zq", [P, KA * T], F32), ("cv", [P, KA, T + 2], F32),
             ("cinp", [P, KA, T + 4], F32),
             ("zk", [P, T + WINDOW], F32),
             ("zv", [P, T], F32), ("v_band", [P, NCH, P], F32),
             ("probs", [P, 2, 2, 3 * CHUNK], F32), ("probs_t", [P, 2, 4, P], F32),
             ("k_cache", [P, P], F32), ("v_cache", [P, P], F32), ("k_new", [P, P], F32),
             ("k_own", [DEC, P], F32), ("v_own", [DEC, P], F32),
             ("conv_rows", [P, 2, 2, KA], F32), ("conv_new", [4 * KA, P], F32),
             ("rmix", [P, 2, HT], F32), ("ssm", [P, 4, HT], F32),
             ("sinks", [P, 8], F32), ("sink", [P, 3, 2], F32), ("nsink", [P, 3, 2], F32),
             ("mx", [P, 2, 2], F32), ("nm", [P, 2, 2], F32), ("se", [P, 2, 2], F32),
             ("es", [P, 2, 2], F32), ("rs", [P, 2, 2], F32), ("den", [P, 2, 2], F32)])
        _, m_lo, y_out = overlay([("pad_m_hi", [P, KD, T], F32), ("m_lo", [P, KD, T], F32R),
                                  ("y_out", [P, KD, T], F32)])
        pT_hi, pT_lo, y_ple, p_tok, out_tok = overlay([
            ("pT_hi", [P, 2 * KP, T], F32R), ("pT_lo", [P, 2 * KP, T], F32R), ("y_ple", [P, KD, T], F32),
            ("p_tok", [P, XT, T], F32), ("out_tok", [P, XT, D], F32)])
        h_hi = sb("h_hi", [P, KF, T], F32R)
        h_lo = sb("h_lo", [P, KF, T], F32R)

        bank = ctx.enter_context(nc.psum_tensor("bank", [P, 4, 512], F32))
        misc = ctx.enter_context(nc.psum_tensor("misc", [P, 4, 512], F32))
        bO, bS, bT = misc[:, 1, :], misc[:, 2, :], misc[:, 3, :]

        w_loaded = [sem(f"w_loaded{s}") for s in range(SLOTS)]
        hi_made, lo_made, half_used = sem("hi_made"), sem("lo_made"), sem("half_used")
        unit_done = sem("unit_done")
        x_in = [sem(f"x_in{i}") for i in range(XT)]
        g_in, cache_in, sink_in, p_in = sem("g_in"), sem("cache_in"), sem("sink_in"), sem("p_in")
        consts, turned_g, g_made = sem("consts"), sem("turned_g"), sem("g_made")
        x_turned, r_loaded = sem("x_turned"), sem("r_loaded")
        y_scaled, r_ready, x_hi_made, x_ready = sem("y_scaled"), sem("r_ready"), sem("x_hi_made"), sem("x_ready")
        squared, summed, sum_done = sem("squared"), sem("summed"), sem("sum_done")
        rooted, inverted = sem("rooted"), sem("inverted")
        g_scaled, gate_act, u_scaled = sem("g_scaled"), sem("gate_act"), sem("u_scaled")
        h_made, h_hi_made = sem("h_made"), sem("h_hi_made")
        h_ready = [sem("h_readyA"), sem("h_readyB")]
        y_ready = sem("y_ready")
        z_ready, z_part, conv_step = sem("z_ready"), sem("z_part"), sem("conv_step")
        rows_made, padded, sinks_made = sem("rows_made"), sem("padded"), sem("sinks_made")
        turned_v, band_ready, conv_turned, conv_out = sem("turned_v"), sem("band_ready"), sem("conv_turned"), sem("conv_out")
        scored, max_made, neg_max, sink_arg = sem("scored"), sem("max_made"), sem("neg_max"), sem("sink_arg")
        exp_made, den_made, den_inv, probs_ready = sem("exp_made"), sem("den_made"), sem("den_inv"), sem("probs_ready")
        turned_p, probs_turned, pv_done, attn_ready = sem("turned_p"), sem("probs_turned"), sem("pv_done"), sem("attn_ready")
        m_scaled, m_hi_made, m_ready = sem("m_scaled"), sem("m_hi_made"), sem("m_ready")
        p_turned, p_hi_made, p_ready = sem("p_turned"), sem("p_hi_made"), sem("p_ready")
        o_turned, o_by_act, o_by_dve = sem("o_turned"), sem("o_by_act"), sem("o_by_dve")
        stored, state_stored = sem("stored"), sem("state_stored")

        MIX_UNITS = [(m, h) for g in range(0, len(MIX), 4) for h in (A, B) for m in MIX[g:g + 4]]

        def task_keys(d):
            c = TASKS[d][0]
            return WINDOW + DEC if c == "sample" else min(c + 1, 3) * CHUNK

        def segments(d):
            c = TASKS[d][0]
            if c == "sample":
                return [(0, WINDOW, 0, v_cache[:]), (WINDOW, DEC, 1, v_own[:])]
            if c == 0:
                return [(0, CHUNK, 1, v_band[0:CHUNK, 0])]
            if c == 1:
                return [(0, P, 0, v_band[:, 0])]
            return [(0, P, 0, v_band[:, c - 2]), (P, CHUNK, 1, v_band[0:CHUNK, c])]

        up = {s: t[w][0].rearrange("(k p) (h f c) -> h f p k c", p=P, h=2, c=P)
              for s, w in (("up1", "w_ffn1_gate_up"), ("up2", "w_ffn2_gate_up"))}
        down = {s: t[w][0].rearrange("(j k p) (m c) -> m j p k c", j=2, p=P, c=P)
                for s, w in (("down1", "w_ffn1_down"), ("down2", "w_ffn2_down"))}
        w_in = t["w_in"][0].rearrange("(k p) n -> p k n", p=P)
        w_out, w_gate, w_proj = t["w_out"][0], t["w_ple_gate"][0], t["w_ple_proj"][0]

        def chunk_loads(c):
            s, j, slot = stage_of[c], c - C0[stage_of[c]], raw[:, c % SLOTS]
            cols = slice(j * P, j * P + P)
            if s == "mix":
                kind = MIX[j]
                if kind[0] == "q":
                    n = int(kind[1])
                    return [(slot[:, 0:KD, e * DH:(e + 1) * DH],
                             w_in[:, :, e * DA // 2 + n * DH:e * DA // 2 + (n + 1) * DH]) for e in range(2)]
                at = {"k": DA, "v": DA + P}.get(kind)
                if at is None:
                    at = VE + "bcx".index(kind[0]) * DA + int(kind[1]) * P
                return [(slot[:, 0:KD, :], w_in[:, :, at:at + P])]
            if s == "out":
                return [(slot[e * DH:(e + 1) * DH, 0:KA, :],
                         w_out[e * DA // 2:(e + 1) * DA // 2, cols].rearrange("(k p) n -> p k n", p=DH))
                        for e in range(2)] + \
                       [(slot[:, KA:KD, :], w_out[DA:D, cols].rearrange("(k p) n -> p k n", p=P))]
            return [(slot[:, 0:KD, :], w_gate[:, cols].rearrange("(k p) n -> p k n", p=P)),
                    (slot[:, KD:KD + KP, :], w_proj[:, cols].rearrange("(k p) n -> p k n", p=P))]

        def used(c):
            s, j = stage_of[c], c - C0[stage_of[c]]
            if s[:4] == "down":
                i, m = j // 4, j % 4 // 2
                if j % 2 == 0:
                    return half_used, HALF0[s] + 2 * i + m + 1, 2
                return unit_done, U0[s] + 4 * i + 2 + m + 1, 4
            if s == "ple":
                return unit_done, U0[s] + 4 * PLE_UNITS.index((j // 2, B)) + 2 + j % 2 + 1, 8
            i, pos = divmod(j, 4)
            rest = min(4, len(MIX) - 4 * i) if s == "mix" else 4
            return unit_done, U0[s] + 8 * i + rest + pos + 1, 8

        def psum(n):
            return bank[:, n % 4, 0:HT]

        def half(tile, k, h):
            return tile[:, k, h * HT:(h + 1) * HT]

        def gain(name, k):
            return gT[:, COL[name] + k:COL[name] + k + 1]

        def p_parts(dst, n):
            if n == KP:
                src = misc[:, 2, 0:KP * DEC].rearrange("p (k n) -> p k n", k=KP)
                return [(dst[:].rearrange("p (k h) t -> p h k t", h=2)[:, B, :, TB:HT], src)]
            return [(dst[:, 2 * n, 0:HT], misc[:, 2 + n, 0:HT]), (dst[:, 2 * n + 1, 0:TB], misc[:, 2 + n, HT:SEQ])]

        def out_banks(tt):
            return (misc[:, 2:4], bank[:, 0:2], bank[:, 2:4], misc[:, 2:4], bank[:, 0:2])[tt]

        def out_part(tt, part):
            n = P if tt < XT - 1 else DEC
            return out_tok[0:n, tt, part * D // 2:(part + 1) * D // 2], out_banks(tt)[0:n, part, :]

        def sum_half(n):
            return n if n < 2 else n % 2 if n >= SUM0["ple"] else (n - 2) // 2 % 2

        def sum_place(n):
            return 0 if SUM0["mix"] <= n < SUM0["out"] else sum_half(n)

        def sum_bank(n):
            return misc[:, sum_place(n), 0:HT]

        block = ctx.enter_context(nc.Block())

        @block.sync
        def _(sp):
            def load_up(s, i):
                for j in range(4):
                    c = C0[s] + j
                    if isinstance(i, int):
                        if c + 4 * i >= SLOTS:
                            sp.wait_ge(lo_made, c + 4 * i - SLOTS + 1)
                    else:
                        sp.wait_ge(lo_made, i * 4 + (c - SLOTS + 1))
                    sp.dma_start(raw[:, c % SLOTS, 0:KD, :], up[s][j % 2, i * 2 + j // 2])\
                        .then_inc(w_loaded[c % SLOTS], 16)

            def load_down(s, i):
                for j in range(4):
                    c = C0[s] + j
                    sp.wait_ge(lo_made, i * 4 + (c - SLOTS + 1))
                    sp.dma_start(raw[:, c % SLOTS], down[s][i * 2 + j // 2, j % 2])\
                        .then_inc(w_loaded[c % SLOTS], 16)

            def load_short(cs):
                for c in cs:
                    sp.wait_ge(lo_made, c - SLOTS + 1)
                    for dst, src in chunk_loads(c):
                        sp.dma_start(dst, src).then_inc(w_loaded[c % SLOTS], 16)

            for i in range(XT - 1):
                sp.dma_start(x_tok[:, i, :], t["x_prompt"][0, i * P:(i + 1) * P, :]).then_inc(x_in[i], 16)
            sp.dma_start(x_tok[0:DEC, XT - 1, :], t["x_sample"][0]).then_inc(x_in[XT - 1], 16)
            for s, d in (("up1", "down1"), ("up2", "down2")):
                load_up(s, 0)
                with sp.Fori(1, UP_GROUPS) as i:
                    load_up(s, i)
                with sp.Fori(0, DOWN_GROUPS) as i:
                    load_down(d, i)
                if s == "up1":
                    load_short(range(C0["mix"], C0["up2"]))
            load_short(range(C0["ple"], C0["ple"] + SLOTS))
            sp.wait_ge(unit_done, U0["ple"] - 2)
            sp.dma_start(p_tok[:, 0:XT - 1, 0:KP * P], t["p_prompt"][0, 0].rearrange("(i p) n -> p i n", p=P))\
                .then_inc(p_in, 16)
            sp.dma_start(p_tok[0:DEC, XT - 1, 0:KP * P], t["p_sample"][0, 0]).then_inc(p_in, 16)
            load_short(range(C0["ple"] + SLOTS, NCHUNK))
            for i in range(XT):
                n = P if i < XT - 1 else DEC
                sp.wait_ge(o_by_act, 2 * i + 2 if i < 2 else i + 3)
                if i >= 2:
                    sp.wait_ge(o_by_dve, i - 1)
                dst = t["y_prompt"][0, i * P:(i + 1) * P, :] if i < XT - 1 else t["y_sample"][0]
                sp.dma_start(dst, out_tok[0:n, i, :]).then_inc(stored, 16)
            sp.wait_ge(stored, 16 * XT)

        @block.gpsimd
        def _(pool):
            nc.gpsimd.memset(ones[:], 1.0).then_inc(consts, 1)
            nc.gpsimd.memset(eps[:], EPS).then_inc(consts, 1)
            nc.gpsimd.memset(ident[:], 0.0).then_inc(consts, 1)
            pool.wait_ge(consts, 3)
            nc.gpsimd.affine_select(out=ident[:], in_=ident[:], compare_op=ALU.not_equal, fill=1.0, base=0,
                                    pattern=[[-1, P]], channel_multiplier=1).then_inc(consts, 1)

            def add(s, dst, first, i=0, per=0):
                pool.wait_ge(squared, i * per + (s + 1))
                if first:
                    nc.gpsimd.tensor_copy(dst, sq[:, s % 2, :]).then_inc(summed, 1)
                else:
                    pool.wait_ge(summed, i * per + s)
                    nc.gpsimd.tensor_tensor(dst, dst, sq[:, s % 2, :], ALU.add).then_inc(summed, 1)

            def run(s, h, n, fresh):
                for k in range(n):
                    add(s + k, ssq[:, h, :], fresh and k == 0)

            def groups(s0, per_half, n_groups):
                run(s0, A, per_half, True)
                run(s0 + per_half, B, per_half, True)
                if n_groups > 3:
                    with pool.Fori(1, n_groups - 1) as i:
                        for j in range(2 * per_half):
                            add(s0 + j, ssq[:, j // per_half, :], False, i, 2 * per_half)
                last = s0 + 2 * per_half * (n_groups - 1)
                return last

            def last_group(s, per_half):
                for h in (A, B):
                    run(s, h, per_half, False)
                    run(s + per_half, h, KD, True)
                    s += per_half + KD

            run(SQ0["start"], A, KD, True)
            run(SQ0["start"] + KD, B, KD, True)
            last_group(groups(SQ0["down1"], 2, DOWN_GROUPS), 2)
            pool.wait_ge(unit_done, U0["mix"])
            nc.gpsimd.memset(cinp[:, :, 0:2], 0.0).then_inc(padded, 1)
            at = COL["cache_conv"]
            nc.gpsimd.tensor_copy(cinp[:, :, SEQ + 2:SEQ + 4],
                                  gT[:, at:at + 2 * KA].rearrange("p (r k) -> p k r", r=2)).then_inc(padded, 1)
            for n in range(4):
                for k in range(KA):
                    add(SQ0["mix"] + n * KA + k, ssm[:, n, :], k == 0)
            last_group(groups(SQ0["out"], 4, 2), 4)
            last_group(groups(SQ0["down2"], 2, DOWN_GROUPS), 2)
            for g in range(2):
                for h in (A, B):
                    run(SQ0["ple"] + 8 * g + 4 * h, h, 4, g == 0)

        @block.scalar
        def _(act):
            def split_hi(c, i=0):
                n, s = width_of[c], c % SLOTS
                act.wait_ge(w_loaded[s], i * 16 + loaded_value(c))
                if c >= SLOTS:
                    semaphore, value, per = used(c - SLOTS)
                    act.wait_ge(semaphore, i * per + value)
                nc.scalar.activation(w_hi[:, s, 0:n, :], raw[:, s, 0:n, :], ACT.Copy).then_inc(hi_made, 1)

            def square(src, s, i=0, per=0):
                if s >= 2:
                    act.wait_ge(summed, i * per + (s - 1))
                return nc.scalar.activation(sq[:, s % 2, :], src, ACT.Square)

            def root(n, size):
                act.wait_ge(sum_done, n + 1)
                nc.scalar.activation(sum_bank(n), sum_bank(n), ACT.Sqrt, bias=eps[:], scale=1.0 / size)\
                    .then_inc(rooted, 1)

            def chain(ci, h, s, after={}):
                post, pre = CHAIN[ci]
                if pre is None:
                    return
                for k in range(KD):
                    if post is None:
                        act.wait_ge(r_loaded, k + 1 if h == A else KD + 1)
                    else:
                        act.wait_ge(r_ready, 16 * (ci - 1) + 8 * h + k + 1)
                    nc.scalar.activation(half(x_hi, k, h), half(r, k, h), ACT.Copy, scale=gain(pre, k))\
                        .then_inc(x_hi_made, 1)
                    square(half(r, k, h), s + k).then_inc(squared, 1)
                    if k in after:
                        after[k]()

            def up_gate(s, h, j, i):
                act.wait_ge(g_scaled, i * 4 + (PAIR0[s] + 2 * h + j + 1))
                nc.scalar.activation(tG[:, j, :], tG[:, j, :], ACT.Silu).then_inc(gate_act, 1)

            def up_hi(s, h, j, i):
                p0 = PAIR0[s] + 2 * h + j
                act.wait_ge(h_made, i * 4 + (p0 + 1))
                nc.scalar.activation(half(h_hi, i * 2 + j, h), tU[:, j, :], ACT.Copy).then_inc(h_hi_made, 1)

            def evacuate(u, y_tile, s, i=0):
                act.wait_ge(unit_done, i * 4 + (u + 1))
                square(psum(u), s, i, 4).then_inc(squared, 1)
                nc.scalar.activation(y_tile, psum(u), ACT.Copy).then_inc(y_ready, 1)

            def up_pair(s, h, j, i):
                up_gate(s, h, j, i)
                up_hi(s, h, j, i)

            def second_half(c, step, i=0):
                for j in range(4):
                    split_hi(c + SLOTS + j, i)
                    if j == 1:
                        step(B, 0)
                step(B, 1)

            def group(c, step, i=0):
                step(A, 0), step(A, 1)
                second_half(c, step, i)

            def p_hi(n):
                act.wait_ge(p_turned, n + 1)
                for dst, src in p_parts(pT_hi, n):
                    i = nc.scalar.activation(dst, src, ACT.Copy)
                i.then_inc(p_hi_made, 1)

            def last_group(c, step, ci, s_a, n0, early, with_p=False):
                step(A, 0), step(A, 1)
                root(n0, D)
                split_hi(c + SLOTS)
                chain(ci, A, s_a, {3: lambda: split_hi(c + SLOTS + 1)})
                if with_p:
                    p_hi(0), p_hi(1)
                step(B, 0)
                split_hi(c + SLOTS + 2)
                if with_p:
                    p_hi(2)
                if early:
                    root(n0 + 1, D)
                step(B, 1)
                split_hi(c + SLOTS + 3)
                if not early:
                    root(n0 + 1, D)
                root(n0 + 2, D)

            def up_stage(s, ci, s_b, n_pre):
                g0 = C0[s]
                chain(ci, B, s_b, {4: lambda: up_gate(s, A, 0, 0)} if ci else {})
                if not ci:
                    root(0, D)
                    up_gate(s, A, 0, 0)
                up_gate(s, A, 1, 0)
                up_hi(s, A, 0, 0), up_hi(s, A, 1, 0)
                root(n_pre, D)
                second_half(g0, lambda h, j: up_pair(s, h, j, 0))
                with act.Fori(1, UP_GROUPS - 1) as i:
                    group(g0, lambda h, j: up_pair(s, h, j, i), i)
                last = UP_GROUPS - 1
                group(g0 + 4 * last, lambda h, j: up_pair(s, h, j, last))

            def down_stage(s, ci):
                g0, s0, n0, last = C0[s], SQ0[s], SUM0[s], DOWN_GROUPS - 1

                def step(i):
                    return lambda h, j: evacuate(U0[s] + 2 * h + j, half(y_down, i * 2 + j, h), s0 + 2 * h + j, i)
                group(g0, step(0))
                with act.Fori(1, last) as i:
                    group(g0, step(i), i)
                sl = s0 + 4 * last

                def last_step(h, j):
                    evacuate(U0[s] + 4 * last + 2 * h + j, half(y_down, 2 * last + j, h), sl + h * (2 + KD) + j)

                last_group(g0 + 4 * last, last_step, ci, sl + 2, n0, True, s == "down2")

            gain_rows = [(COL[n], KD, t[n].rearrange("a (k p) -> (a k) p", p=P)) for n in
                         ("norm_ffn1_pre", "norm_ffn1_post", "norm_mix_pre", "norm_mix_post", "norm_ffn2_pre",
                          "norm_ffn2_post", "norm_ple_pre", "norm_ple_post")]
            gain_rows += [(COL["norm_conv_out"], KA, t["norm_conv_out"].rearrange("a (k p) -> (a k) p", p=P)),
                          (COL["conv_w"], 3 * KA, t["conv_w"].rearrange("a j (k p) -> (a j k) p", p=P)),
                          (COL["cache_conv"], 2 * KA, t["cache_conv"].rearrange("a b j (k p) -> (a b j k) p", p=P))]
            for at, n, src in gain_rows:
                act.dma_start(g_rows[at:at + n, :], src).then_inc(g_in, 16)
            at = COL["norm_attn_out"]
            for e in range(2):
                act.dma_start(g_rows[at:at + KA, e * DH:(e + 1) * DH],
                              t["norm_attn_out"][0, e * DA // 2:(e + 1) * DA // 2].rearrange("(k p) -> k p", p=DH))\
                    .then_inc(g_in, 16)
            act.dma_start(t["new_k_sample"][0, 0, 0:WINDOW - DEC], t["cache_attn_k"][0, 0, DEC:WINDOW])\
                .then_inc(state_stored, 16)
            act.dma_start(t["new_v_sample"][0, 0, 0:WINDOW - DEC], t["cache_attn_v"][0, 0, DEC:WINDOW])\
                .then_inc(state_stored, 16)

            act.wait_ge(g_made, 1)
            act.wait_ge(consts, 4)
            chain(0, A, 0)
            for c in range(SLOTS):
                split_hi(c)
            up_stage("up1", 0, KD, 1)
            down_stage("down1", 1)

            def mix_first():
                chain(1, B, SQ0["mix"] - KD)
                root(SUM0["down1"] + 3, D)
                act.wait_ge(unit_done, U0["mix"])
                act.dma_start(k_cache[:], t["cache_attn_k"][0, 0].rearrange("w g d -> w (g d)")).then_inc(cache_in, 16)
                act.dma_start(v_cache[:], t["cache_attn_v"][0, 0].rearrange("w g d -> w (g d)")).then_inc(cache_in, 16)
                act.dma_start(sinks[:], t["attn_sinks"].to_broadcast([P, 8])).then_inc(sink_in, 16)

            def softmax_exp(d):
                b, n = d % 2, task_keys(d)
                act.wait_ge(neg_max, d + 1)
                for g in range(2):
                    nc.scalar.activation(probs[:, b, g, 0:n], bS[:, g * 192:g * 192 + n], ACT.Exp,
                                         bias=nm[:, b, g:g + 1], scale=SCALE, accum_out=rs[:, b, g:g + 1])
                act.wait_ge(sink_arg, d + 1)
                nc.scalar.activation(es[:, b, :], se[:, b, :], ACT.Exp).then_inc(exp_made, 1)

            def copy_probs(d):
                act.wait_ge(turned_p, d + 1)
                segs = segments(d)
                for n, (_, rows, place, _) in enumerate(segs):
                    a = nc.scalar.activation(
                        probs_t[0:rows, d % 2, 2 * place:2 * place + 2, :],
                        bT[0:rows, 2 * place * P:(2 * place + 2) * P].rearrange("p (g q) -> p g q", g=2), ACT.Copy)
                a.then_inc(probs_turned, 1)

            def mix_squares(n):
                kind, h = n % 2, n // 2
                for k in range(KA):
                    if kind:
                        act.wait_ge(z_ready, MIX_UNITS.index((f"b{k}", h)) + 1)
                    else:
                        act.wait_ge(attn_ready, 10 if h == A else NTASK)
                    square(half(ac, kind * KA + k, h), SQ0["mix"] + n * KA + k).then_inc(squared, 1)

            def mix_his(n):
                kind, h = n % 2, n // 2
                for k in range(KA):
                    act.wait_ge(m_scaled, n * KA + k + 1)
                    nc.scalar.activation(half(m_hi, kind * KA + k, h), half(ac, kind * KA + k, h), ACT.Copy,
                                         scale=gain("norm_conv_out" if kind else "norm_attn_out", k))\
                        .then_inc(m_hi_made, 1)

            def mix_root(n):
                root(SUM0["mix"] + n, DA)

            c0 = C0["mix"]
            mix_first()
            for j in range(4):
                split_hi(c0 + SLOTS + j)
            act.wait_ge(turned_v, 1)
            nc.scalar.activation(v_band[:, 0:4, :], bS.rearrange("p (m c) -> p m c", m=4), ACT.Copy).then_inc(band_ready, 1)
            act.wait_ge(turned_v, 2)
            nc.scalar.activation(v_band[:, 4:7, :], bT[:, 0:3 * P].rearrange("p (m c) -> p m c", m=3), ACT.Copy)
            nc.scalar.activation(v_band[0:CHUNK, 7, :], bT[0:CHUNK, 3 * P:4 * P], ACT.Copy).then_inc(band_ready, 1)
            act.wait_ge(turned_v, 3)
            nc.scalar.activation(zk[:, SEQ:SEQ + WINDOW], bS[:, 0:P], ACT.Copy)
            nc.scalar.activation(k_new[:], bS[:, P:2 * P], ACT.Copy)
            nc.scalar.activation(v_own[:], bS[0:DEC, 2 * P:3 * P], ACT.Copy)
            nc.scalar.activation(k_own[:], bS[0:DEC, 3 * P:4 * P], ACT.Copy).then_inc(band_ready, 1)
            act.wait_ge(band_ready, 3)
            flat = "a b w g d -> (a b w) (g d)"
            act.dma_start(t["new_k_prompt"].rearrange(flat), k_new[:]).then_inc(state_stored, 16)
            act.dma_start(t["new_v_prompt"].rearrange(flat), v_band[:, NCH - 2, :]).then_inc(state_stored, 16)
            act.dma_start(t["new_k_sample"].rearrange(flat)[WINDOW - DEC:WINDOW, :], k_own[:]).then_inc(state_stored, 16)
            act.dma_start(t["new_v_sample"].rearrange(flat)[WINDOW - DEC:WINDOW, :], v_own[:]).then_inc(state_stored, 16)
            for j in range(4):
                split_hi(c0 + 2 * SLOTS + j)
            for v in range(20):
                g, j = divmod(v, 8)
                if v < 16 and j >= 4:
                    split_hi(c0 + 12 + 4 * g + j - 4)
                if v >= 18:
                    split_hi(c0 + 20 + v - 18)
                if 1 <= v <= NTASK:
                    copy_probs(v - 1)
                if v < NTASK:
                    softmax_exp(v)
                if v == 12:
                    mix_squares(0)
                if v == 13:
                    mix_root(0)
                if v == 14:
                    mix_his(0)
                if v == 17:
                    mix_squares(1)
                if v == 18:
                    mix_root(1)
                    mix_his(1)
                    mix_squares(2)
            mix_squares(3)
            act.wait_ge(conv_turned, 1)
            nc.scalar.activation(conv_new[:], bT[0:4 * KA, 0:P], ACT.Copy).then_inc(conv_out, 1)
            act.wait_ge(conv_out, 1)
            rows = "a b j (k p) -> (a b j k) p"
            act.dma_start(t["new_conv_prompt"].rearrange(rows, p=P), conv_new[0:2 * KA, :]).then_inc(state_stored, 16)
            act.dma_start(t["new_conv_sample"].rearrange(rows, p=P), conv_new[2 * KA:4 * KA, :]).then_inc(state_stored, 16)
            for n in (2, 3):
                mix_root(n)
                mix_his(n)

            def out_evacuate(i, h, j):
                for m in (2 * j, 2 * j + 1):
                    evacuate(U0["out"] + 8 * i + 4 * h + m, half(y_out, 4 * i + m, h),
                             SQ0["out"] + 8 * i + (4 + KD * i) * h + m)

            group(C0["out"], lambda h, j: out_evacuate(0, h, j))
            last_group(C0["out"] + 4, lambda h, j: out_evacuate(1, h, j), 2, SQ0["out"] + 12, SUM0["out"], False)

            act.wait_ge(state_stored, 16 * 8)
            up_stage("up2", 2, SQ0["down2"] - KD, SUM0["out"] + 3)
            down_stage("down2", 3)

            def ple_gate(g):
                for m in range(2):
                    act.wait_ge(g_scaled, 4 * KF + 2 * g + m + 1)
                    nc.scalar.activation(tG[:, m, :], tG[:, m, :], ACT.Sigmoid).then_inc(gate_act, 1)

            def ple_square(g):
                i, h = PLE_UNITS[g]
                for m in range(2):
                    act.wait_ge(h_made, 4 * KF + 2 * g + m + 1)
                    square(half(y_ple, 2 * i + m, h), SQ0["ple"] + 2 * g + m).then_inc(squared, 1)

            chain(3, B, SQ0["ple"] - KD, {3: lambda: ple_gate(0)})
            ple_square(0)
            ple_gate(1)
            ple_square(1)
            root(SUM0["down2"] + 3, D)
            for g in range(2, 2 * DOWN_GROUPS):
                ple_gate(g)
                ple_square(g)
                if g < 4:
                    for m in range(2):
                        split_hi(C0["ple"] + 2 * g + m)
                if g == 5:
                    root(SUM0["ple"], D)

            def copy_out(tt, parts):
                for part in parts:
                    act.wait_ge(o_turned, tt + 1)
                    dst, src = out_part(tt, part)
                    nc.scalar.activation(dst, src, ACT.Copy).then_inc(o_by_act, 1)
            copy_out(0, (0, 1))
            root(SUM0["ple"] + 1, D)
            copy_out(1, (0, 1))
            for tt in range(2, XT):
                copy_out(tt, (0,))
            act.wait_ge(state_stored, 16 * 8)

        @block.vector
        def _(dve):
            def split_lo(c, i=0):
                n, s = width_of[c], c % SLOTS
                dve.wait_ge(hi_made, i * 4 + (c + 1))
                nc.vector.tensor_tensor(w_lo[:, s, 0:n, :], raw[:, s, 0:n, :], w_hi[:, s, 0:n, :].bitcast(F32),
                                        ALU.subtract).then_inc(lo_made, 1)

            def invert(n, dst):
                dve.wait_ge(rooted, n + 1)
                nc.vector.reciprocal(dst, sum_bank(n)).then_inc(inverted, 1)
                dve.wait_ge(inverted, n + 1)

            def chain_r(ci, h, y, n, after={}):
                post, e0 = CHAIN[ci][0], 16 * (ci - 1) + 8 * h

                def scale(k):
                    nc.vector.tensor_tensor(half(y, k, h), sum_bank(n), half(y, k, h), ALU.mult).then_inc(y_scaled, 1)
                invert(n, sum_bank(n))
                scale(0)
                for k in range(KD):
                    if k + 1 < KD:
                        scale(k + 1)
                    dve.wait_ge(y_scaled, e0 + k + 1)
                    nc.vector.scalar_tensor_tensor(half(r, k, h), half(y, k, h), gain(post, k), half(r, k, h),
                                                   ALU.mult, ALU.add).then_inc(r_ready, 1)
                    if k in after:
                        after[k]()

            def chain_lo(ci, h, ks=range(KD)):
                for k in ks:
                    dve.wait_ge(x_hi_made, 16 * ci + 8 * h + k + 1)
                    nc.vector.scalar_tensor_tensor(half(x_lo, k, h), half(r, k, h), gain(CHAIN[ci][1], k),
                                                   half(x_hi, k, h).bitcast(F32), ALU.mult, ALU.subtract)\
                        .then_inc(x_ready, 1)

            def up_scale(s, h, j, i):
                u = U0[s] + 4 * h + 2 * j
                dve.wait_ge(unit_done, i * 8 + (u + 1))
                nc.vector.tensor_tensor(tG[:, j, :], psum(u), rpre[:, h, :], ALU.mult).then_inc(g_scaled, 1)
                dve.wait_ge(unit_done, i * 8 + (u + 2))
                nc.vector.tensor_tensor(tU[:, j, :], psum(u + 1), rpre[:, h, :], ALU.mult).then_inc(u_scaled, 1)

            def up_hidden(s, h, j, i):
                p0 = PAIR0[s] + 2 * h + j
                dve.wait_ge(gate_act, i * 4 + (p0 + 1))
                dve.wait_ge(u_scaled, i * 4 + (p0 + 1))
                nc.vector.tensor_tensor(tU[:, j, :], tG[:, j, :], tU[:, j, :], ALU.mult).then_inc(h_made, 1)
                dve.wait_ge(h_hi_made, i * 4 + (p0 + 1))
                nc.vector.tensor_tensor(half(h_lo, i * 2 + j, h), tU[:, j, :], half(h_hi, i * 2 + j, h).bitcast(F32),
                                        ALU.subtract).then_inc(h_ready[h], 1)

            def up_pair(s, h, j, i):
                up_scale(s, h, j, i)
                up_hidden(s, h, j, i)

            def second_half(c, step=None, i=0):
                for j in range(4):
                    split_lo(c + SLOTS + j, i)
                    if step and j == 1:
                        step(B, 0)
                if step:
                    step(B, 1)

            def group(c, step, i=0):
                step(A, 0), step(A, 1)
                second_half(c, step, i)

            def up_stage(s, ci, y, n_pre):
                g0, last = C0[s], UP_GROUPS - 1
                if ci:
                    chain_r(ci, B, y, n_pre - 1, {4: lambda: up_scale(s, A, 0, 0)})
                else:
                    invert(0, rpre[:, A, :])
                    up_scale(s, A, 0, 0)
                up_scale(s, A, 1, 0)
                up_hidden(s, A, 0, 0), up_hidden(s, A, 1, 0)
                if ci:
                    chain_lo(ci, B)
                invert(n_pre, rpre[:, B, :])
                second_half(g0, lambda h, j: up_pair(s, h, j, 0))
                with dve.Fori(1, last) as i:
                    group(g0, lambda h, j: up_pair(s, h, j, i), i)
                group(g0 + 4 * last, lambda h, j: up_pair(s, h, j, last))

            def p_lo(n):
                dve.wait_ge(p_hi_made, n + 1)
                for (dst, src), (hi, _) in zip(p_parts(pT_lo, n), p_parts(pT_hi, n)):
                    i = nc.vector.tensor_tensor(dst, src, hi.bitcast(F32), ALU.subtract)
                i.then_inc(p_ready, 1)

            def last_group(c, ci, y, n0, early, with_p=False):
                chain_r(ci, A, y, n0)
                split_lo(c + SLOTS), split_lo(c + SLOTS + 1)
                if with_p:
                    p_lo(0), p_lo(1)
                if not early:
                    chain_lo(ci, A)
                split_lo(c + SLOTS + 2)
                if with_p:
                    p_lo(2)
                if early:
                    invert(n0 + 1, rpre[:, A, :])
                    chain_lo(ci, A, range(0, KD // 2))
                split_lo(c + SLOTS + 3)
                if early:
                    chain_lo(ci, A, range(KD // 2, KD))
                else:
                    invert(n0 + 1, rpre[:, A, :])

            def down_stage(s, ci):
                g0, last = C0[s], DOWN_GROUPS - 1
                second_half(g0)
                with dve.Fori(1, last) as i:
                    second_half(g0, None, i)
                last_group(g0 + 4 * last, ci, y_down, SUM0[s], True, s == "down2")

            dve.wait_ge(turned_g, 1)
            nc.vector.tensor_copy(gT[:], bank[:, 0, 0:nrows]).then_inc(g_made, 1)
            dve.wait_ge(g_made, 1)
            for n in ("norm_ffn1_post", "norm_ffn2_post"):
                g = gT[:, COL[n]:COL[n] + KD]
                nc.vector.tensor_scalar(g, g, 0.5, None, ALU.mult).then_inc(g_made, 1)
            for k in range(KD):
                dve.wait_ge(x_turned, k + 1)
                nc.vector.tensor_copy(r[:, k, 0:SEQ], misc[:, k % 3, :]).then_inc(r_loaded, 1)
            dve.wait_ge(x_turned, KD + 1)
            nc.vector.tensor_copy(r[:, :, SEQ:T], bT[:, 0:KD * DEC].rearrange("p (k n) -> p k n", k=KD))\
                .then_inc(r_loaded, 1)
            dve.wait_ge(r_loaded, KD + 1)
            chain_lo(0, A)
            for c in range(SLOTS):
                split_lo(c)
            chain_lo(0, B)
            dve.wait_ge(g_made, 3)
            up_stage("up1", 0, None, 1)
            down_stage("down1", 1)

            count = {"part": 0, "conv": 0}

            def evacuate(v):
                (tile, h), u = MIX_UNITS[v], U0["mix"] + v
                kind, j = tile[0], int(tile[1:] or 0)
                dve.wait_ge(unit_done, u + 1)
                ps, scale = psum(u), rpre[:, h, :]
                if kind == "v":
                    nc.vector.tensor_tensor(zv[:, h * HT:(h + 1) * HT], ps, scale, ALU.mult).then_inc(z_ready, 1)
                    return
                if kind == "q":
                    q_prompt = zq[:, 0:KA * SEQ].rearrange("p (c k n) -> p k c n", k=KA, n=CHUNK)[:, j]
                    q_sample = zq[:, KA * SEQ:KA * T].rearrange("p (k n) -> p k n", k=KA)[:, j]
                    whole, rest = divmod(HT, CHUNK)
                    if h == A:
                        pieces = [(0, whole * CHUNK, q_prompt[:, 0:whole, :]),
                                  (whole * CHUNK, HT, q_prompt[:, whole, 0:rest])]
                    else:
                        pieces = [(0, CHUNK - rest, q_prompt[:, whole, rest:CHUNK]),
                                  (CHUNK - rest, TB, q_prompt[:, whole + 1:NCH, :]), (TB, HT, q_sample)]
                    for a, b, dst in pieces:
                        src, by = ps[:, a:b], scale[:, a:b]
                        if len(dst.shape) == 3:
                            src, by = (z.rearrange("p (c n) -> p c n", n=CHUNK) for z in (src, by))
                        i = nc.vector.tensor_tensor(dst, src, by, ALU.mult)
                    i.then_inc(z_ready, 1)
                    return
                ranges = [(0, HT)] if h == A else [(0, TB), (TB, HT)]
                if kind in "xb":
                    tmp = (tG if kind == "x" else tU)[:, count["part"] % 2, :]
                    nc.vector.tensor_tensor(tmp, ps, scale, ALU.mult).then_inc(z_part, 1)
                    count["part"] += 1
                    dve.wait_ge(z_part, count["part"])
                if kind == "x":
                    dve.wait_ge(z_ready, MIX_UNITS.index((f"c{j}", h)) + 1)
                if kind == "b":
                    dve.wait_ge(conv_step, count[f"cv{j}{h}"])
                for n, (a, b) in enumerate(ranges):
                    token = h * HT + a
                    pad = 2 if token < SEQ else 4
                    if kind == "k":
                        at = token if token < SEQ else SEQ + WINDOW
                        i = nc.vector.tensor_tensor(zk[:, at:at + b - a], ps[:, a:b], scale[:, a:b], ALU.mult)
                    if kind == "c":
                        i = nc.vector.tensor_tensor(cinp[:, j, token + pad:token + pad + b - a], ps[:, a:b],
                                                    scale[:, a:b], ALU.mult)
                    if kind == "x":
                        dst = cinp[:, j, token + pad:token + pad + b - a]
                        i = nc.vector.tensor_tensor(dst, dst, tmp[:, a:b], ALU.mult)
                    if kind == "b":
                        src = cv[:, j, token + pad - 2:token + pad - 2 + b - a]
                        i = nc.vector.tensor_tensor(ac[:, KA + j, token:token + b - a], src, tmp[:, a:b], ALU.mult)
                i.then_inc(z_ready, 1)
                if kind == "x":
                    if count["conv"] == 0:
                        dve.wait_ge(padded, 2)
                    dve.wait_ge(z_ready, v + 1)
                    a, n = (0, HT) if h == A else (HT, T + 2 - HT)
                    dst = cv[:, j, a:a + n]
                    for tap in range(3):
                        src, w = cinp[:, j, a + tap:a + tap + n], gain("conv_w", tap * KA + j)
                        if tap == 0:
                            i = nc.vector.tensor_scalar(dst, src, w, None, ALU.mult)
                        else:
                            dve.wait_ge(conv_step, count["conv"])
                            i = nc.vector.scalar_tensor_tensor(dst, src, w, dst, ALU.mult, ALU.add)
                        i.then_inc(conv_step, 1)
                        count["conv"] += 1
                    count[f"cv{j}{h}"] = count["conv"]

            def softmax_max(d):
                b, n, p = d % 2, task_keys(d), 2 if TASKS[d][0] == "sample" else TASKS[d][1]
                dve.wait_ge(scored, 2 * d + 2)
                nc.vector.reduce_max(mx[:, b, :], bS[:, 0:384].rearrange("p (g s) -> p g s", g=2)[:, :, 0:n], AX_X)\
                    .then_inc(max_made, 1)
                dve.wait_ge(max_made, d + 1)
                nc.vector.scalar_tensor_tensor(nm[:, b, :], mx[:, b, :], -SCALE, nsink[:, p, :], ALU.mult, ALU.min)\
                    .then_inc(neg_max, 1)
                dve.wait_ge(neg_max, d + 1)
                nc.vector.tensor_tensor(se[:, b, :], sink[:, p, :], nm[:, b, :], ALU.add).then_inc(sink_arg, 1)

            def softmax_scale(d):
                b, n = d % 2, task_keys(d)
                dve.wait_ge(exp_made, d + 1)
                nc.vector.tensor_tensor(den[:, b, :], rs[:, b, :], es[:, b, :], ALU.add).then_inc(den_made, 1)
                dve.wait_ge(den_made, d + 1)
                nc.vector.reciprocal(den[:, b, :], den[:, b, :]).then_inc(den_inv, 1)
                dve.wait_ge(den_inv, d + 1)
                for g in range(2):
                    i = nc.vector.tensor_scalar(probs[:, b, g, 0:n], probs[:, b, g, 0:n], den[:, b, g:g + 1], None,
                                                ALU.mult)
                i.then_inc(probs_ready, 1)

            def attention_out(d):
                c, p = TASKS[d]
                dve.wait_ge(pv_done, d + 1)
                if c == "sample":
                    dst = ac[:, 0:KA, SEQ:T]
                else:
                    dst = ac[:, 2 * p:2 * p + 2, c * CHUNK:(c + 1) * CHUNK]
                nc.vector.tensor_copy(dst, bO[:, 0:P].rearrange("p (t n) -> p t n", n=dst.shape[2]))\
                    .then_inc(attn_ready, 1)

            def mix_norm(n):
                kind, h = n % 2, n // 2
                name = "norm_conv_out" if kind else "norm_attn_out"
                invert(SUM0["mix"] + n, rmix[:, kind, :])

                def scale(k):
                    src = half(ac, kind * KA + k, h)
                    nc.vector.tensor_tensor(src, src, rmix[:, kind, :], ALU.mult).then_inc(m_scaled, 1)
                scale(0)
                for k in range(KA):
                    if k + 1 < KA:
                        scale(k + 1)
                    dve.wait_ge(m_hi_made, n * KA + k + 1)
                    dve.wait_ge(m_scaled, n * KA + k + 1)
                    nc.vector.scalar_tensor_tensor(half(m_lo, kind * KA + k, h), half(ac, kind * KA + k, h), gain(name, k),
                                                   half(m_hi, kind * KA + k, h).bitcast(F32), ALU.mult, ALU.subtract)\
                        .then_inc(m_ready, 1)

            c0 = C0["mix"]
            chain_r(1, B, y_down, SUM0["down1"] + 2, {4: lambda: (evacuate(0), evacuate(1))})
            for v in range(2, 16):
                evacuate(v)
                if v == 3:
                    chain_lo(1, B)
                    invert(SUM0["down1"] + 3, rpre[:, B, :])
                if v % 8 >= 4:
                    split_lo(c0 + SLOTS + 4 * (v // 8) + v % 4)
            dve.wait_ge(sink_in, 16)
            for e in range(2):
                rows = slice(e * DH, (e + 1) * DH)
                nc.vector.tensor_copy(sink[rows, 0:2, :],
                                      sinks[rows, :].rearrange("r (g p e) -> r e p g", g=2, p=2)[:, e]).then_inc(sinks_made, 1)
            for q in range(4):
                rows = slice(q * DEC, (q + 1) * DEC)
                nc.vector.tensor_copy(sink[rows, 2, :], sinks[rows, q:8:4]).then_inc(sinks_made, 1)
            dve.wait_ge(sinks_made, 6)
            nc.vector.tensor_scalar(nsink[:], sink[:], -1.0, None, ALU.mult).then_inc(sinks_made, 1)
            dve.wait_ge(sinks_made, 7)
            for v in range(20):
                evacuate(16 + v)
                if v < NTASK:
                    softmax_max(v)
                if v < 16 and v % 8 >= 4:
                    split_lo(c0 + 12 + 4 * (v // 8) + v % 8 - 4)
                if v >= 18:
                    split_lo(c0 + 20 + v - 18)
                if v == 15:
                    for s, at in enumerate((SEQ, T + 2)):
                        i = nc.vector.tensor_copy(conv_rows[:, s], cinp[:, :, at:at + 2].rearrange("p k r -> p r k"))
                    i.then_inc(rows_made, 1)
                if 2 <= v < NTASK + 2:
                    attention_out(v - 2)
                if v < NTASK:
                    softmax_scale(v)
                if v == 14:
                    mix_norm(0)
                if v == 18:
                    mix_norm(1)
            mix_norm(2)
            mix_norm(3)

            second_half(C0["out"])
            last_group(C0["out"] + 4, 2, y_out, SUM0["out"], False)

            up_stage("up2", 2, y_out, SUM0["out"] + 3)
            down_stage("down2", 3)

            def ple_gate(g):
                dve.wait_ge(h_made, PAIR0["ple"] + 2 * g)
                for m in range(2):
                    u = U0["ple"] + 4 * g + m
                    dve.wait_ge(unit_done, u + 1)
                    nc.vector.tensor_tensor(tG[:, m, :], psum(u), rpre[:, PLE_UNITS[g][1], :], ALU.mult)\
                        .then_inc(g_scaled, 1)

            def ple_mul(g):
                i, h = PLE_UNITS[g]
                for m in range(2):
                    u = U0["ple"] + 4 * g + 2 + m
                    dve.wait_ge(gate_act, PAIR0["ple"] + 2 * g + m + 1)
                    dve.wait_ge(unit_done, u + 1)
                    nc.vector.tensor_tensor(half(y_ple, 2 * i + m, h), psum(u), tG[:, m, :], ALU.mult).then_inc(h_made, 1)

            chain_r(3, B, y_down, SUM0["down2"] + 2, {3: lambda: ple_gate(0)})
            ple_mul(0)
            ple_gate(1)
            chain_lo(3, B)
            ple_mul(1)
            invert(SUM0["down2"] + 3, rpre[:, B, :])
            for g in range(2, 2 * DOWN_GROUPS):
                ple_gate(g)
                ple_mul(g)
                if g < 4:
                    for m in range(2):
                        split_lo(C0["ple"] + 2 * g + m)
                if g == 5:
                    chain_r(4, A, y_ple, SUM0["ple"])
            chain_r(4, B, y_ple, SUM0["ple"] + 1)
            for tt in range(2, XT):
                dve.wait_ge(o_turned, tt + 1)
                dst, src = out_part(tt, 1)
                nc.vector.tensor_copy(dst, src).then_inc(o_by_dve, 1)

        @block.tensor
        def _(pe):
            def product(u, tiles, hooks=None, marks=None):
                n = len(tiles)
                for k, (slot, kk, hi, lo) in enumerate(tiles):
                    if hooks and k in hooks:
                        hooks[k]()
                    wh, wl = w_hi[:, slot, kk, :], w_lo[:, slot, kk, :]
                    nc.tensor.matmul(psum(u), wh, hi, start=(k == 0), stop=False)
                    nc.tensor.matmul(psum(u), wh, lo, start=False, stop=False)
                    mm = nc.tensor.matmul(psum(u), wl, hi, start=False, stop=(k == n - 1))
                    if marks and k in marks:
                        mm.then_inc(marks[k], 1)
                mm.then_inc(unit_done, 1)

            def all_sums(n, size=None):
                pe.wait_ge(summed, SUMMED[n])
                last = [m for m in range(n) if sum_place(m) == sum_place(n)]
                if last:
                    pe.wait_ge(inverted, last[-1] + 1)
                k = n - SUM0["mix"]
                src = ssm[:, k, :] if 0 <= k < 4 else ssq[:, sum_half(n), :]
                nc.tensor.matmul(sum_bank(n), ones[:], src, start=True, stop=True).then_inc(sum_done, 1)

            def hi_pass(pair, x_hi, h, wait, hooks={}):
                for k in range(KD):
                    wait(k)
                    if k in hooks:
                        hooks[k]()
                    for u, c, ready in pair:
                        if k == 0:
                            ready()
                        for w in (w_hi, w_lo):
                            nc.tensor.matmul(psum(u), w[:, c % SLOTS, k, :], half(x_hi, k, h),
                                             start=(k == 0 and w is w_hi), stop=False)

            def lo_pass(u, c, x_lo, h, wait=None):
                for k in range(KD):
                    if wait:
                        wait(k)
                    mm = nc.tensor.matmul(psum(u), w_hi[:, c % SLOTS, k, :], half(x_lo, k, h),
                                          start=False, stop=(k == KD - 1))
                mm.then_inc(unit_done, 1)

            def first_units(units, ci, h, hooks_hi={}, hooks_lo={}, second={}):
                hi_pass(units[0:2], x_hi, h, lambda k: pe.wait_ge(x_hi_made, 16 * ci + 8 * h + k + 1), hooks_hi)
                if units[2:4]:
                    hi_pass(units[2:4], x_hi, h, lambda k: None, second)
                for n, (u, c, _) in enumerate(units):
                    lo_pass(u, c, x_lo, h, None if n else lambda k: pe.wait_ge(x_ready, 16 * ci + 8 * h + k + 1))
                    if n in hooks_lo:
                        hooks_lo[n]()

            def x_tiles(slot, h):
                return [(slot, k, half(x_hi, k, h), half(x_lo, k, h)) for k in range(KD)]

            def up_ready(s, i, h, pos):
                if h == A:
                    pe.wait_ge(lo_made, i * 4 + (C0[s] + pos + 1))
                if not (isinstance(i, int) and i == 0 and h == A):
                    pe.wait_ge(g_scaled if pos % 2 == 0 else u_scaled, i * 4 + (PAIR0[s] + 2 * h + pos // 2 - 2 + 1))
                elif s == "up2":
                    pe.wait_ge(y_ready, Y0["out"] + 2 * KD - 3 + pos)

            def up_stage(s, ci, hooks_hi, second, n_pre):
                for h in (A, B):
                    units = [(U0[s] + 4 * h + pos, C0[s] + pos, lambda h=h, pos=pos: up_ready(s, 0, h, pos))
                             for pos in range(4)]
                    if h == A:
                        first_units(units, ci, A, hooks_hi, {}, second)
                    else:
                        first_units(units, ci, B, {}, {0: lambda: all_sums(n_pre)})
                with pe.Fori(1, UP_GROUPS) as i:
                    for h in (A, B):
                        for pos in range(4):
                            up_ready(s, i, h, pos)
                            product(U0[s] + 4 * h + pos, x_tiles((C0[s] + pos) % SLOTS, h))

            def down_group(s, i, up_s, hooks_b={}):
                for h in (A, B):
                    if isinstance(i, int) and i == 0:
                        pe.wait_ge(h_ready[h], KF * (1 if s == "down1" else 2))
                    for m in range(2):
                        u, c = U0[s] + 2 * h + m, C0[s] + 2 * m
                        if h == A:
                            pe.wait_ge(lo_made, i * 4 + (c + 2))
                        if isinstance(i, int) and i == 0:
                            pair = 2 * KF - 2 + h
                            emptied, p0 = (g_scaled, PAIR0[up_s]) if m == 0 else (u_scaled, PAIR0[up_s])
                            pe.wait_ge(emptied, p0 + pair + 1)
                        else:
                            pe.wait_ge(y_ready, i * 4 + (Y0[s] + 2 * h + m - 3))
                        tiles = [((c + k // MAXK) % SLOTS, k % MAXK, half(h_hi, k, h), half(h_lo, k, h))
                                 for k in range(KF)]
                        marks = {MAXK - 1: half_used} if h == B else {}
                        product(u, tiles, hooks_b.get(m) if h == B else None, marks)

            def down_stage(s, up_s, hooks_b):
                last = DOWN_GROUPS - 1
                down_group(s, 0, up_s)
                with pe.Fori(1, last) as i:
                    down_group(s, i, up_s)
                down_group(s, last, up_s, hooks_b)

            def turn(dst, src, n=P):
                return nc.tensor.transpose(dst, src, ident[0:n, 0:n])

            pe.wait_ge(consts, 4)
            pe.wait_ge(g_in, 16 * 13)
            turn(bank[:, 0, 0:nrows], g_rows[:], nrows).then_inc(turned_g, 1)
            for k in range(KD):
                if k >= 3:
                    pe.wait_ge(r_loaded, k - 2)
                for i in range(XT - 1):
                    if k == 0:
                        pe.wait_ge(x_in[i], 16)
                    tr = turn(misc[:, k % 3, i * P:(i + 1) * P], x_tok[:, i, k * P:(k + 1) * P])
                tr.then_inc(x_turned, 1)
            pe.wait_ge(x_in[XT - 1], 16)
            for k in range(KD):
                tr = turn(bT[:, k * DEC:(k + 1) * DEC], x_tok[0:DEC, XT - 1, k * P:(k + 1) * P], DEC)
            tr.then_inc(x_turned, 1)

            up_stage("up1", 0, {}, {6: lambda: all_sums(0)}, 1)
            n0 = SUM0["down1"]
            down_stage("down1", "up1", {0: {5: lambda: all_sums(n0)}, 1: {17: lambda: all_sums(n0 + 1)}})

            def scores(d, g):
                c, p = TASKS[d]
                if g:
                    pe.wait_ge(scored, 2 * d + 1)
                elif d:
                    pe.wait_ge(exp_made, d)
                rows = slice(g * DH, (g + 1) * DH)
                if c == "sample":
                    q, keys = zq[rows, KA * SEQ:KA * T], zk[rows, SEQ:SEQ + WINDOW + DEC]
                else:
                    q = zq[rows, (2 * c + p) * P:(2 * c + p + 1) * P]
                    keys = zk[rows, max(c - 2, 0) * CHUNK:(c + 1) * CHUNK]
                mm = nc.tensor.matmul(bS[:, g * 192:g * 192 + task_keys(d)], q, keys, start=True, stop=True)
                mm.then_inc(scored, 1)

            def turn_probs(d):
                pe.wait_ge(probs_ready, d + 1)
                if d:
                    pe.wait_ge(probs_turned, d)
                for first, rows, place, _ in segments(d):
                    for g in range(2):
                        at = (2 * place + g) * P
                        tr = turn(bT[0:rows, at:at + P], probs[:, d % 2, g, first:first + rows])
                tr.then_inc(turned_p, 1)

            def weigh(d):
                pe.wait_ge(probs_turned, d + 1)
                if d:
                    pe.wait_ge(attn_ready, d)
                segs = segments(d)
                for g in range(2):
                    for n, (_, rows, place, values) in enumerate(segs):
                        mm = nc.tensor.matmul(bO[g * DH:(g + 1) * DH, 0:P], values[:, g * DH:(g + 1) * DH],
                                              probs_t[0:rows, d % 2, 2 * place + g, :],
                                              start=(n == 0), stop=(n == len(segs) - 1))
                mm.then_inc(pv_done, 1)

            def turn_kv(part):
                if part == 0:
                    pe.wait_ge(z_ready, 8)
                    for m in range(4):
                        tr = turn(bS[:, m * P:(m + 1) * P], zv[:, m * CHUNK:m * CHUNK + P])
                    tr.then_inc(turned_v, 1)
                    for m in range(4, 7):
                        tr = turn(bT[:, (m - 4) * P:(m - 3) * P], zv[:, m * CHUNK:m * CHUNK + P])
                    turn(bT[0:CHUNK, 3 * P:4 * P], zv[:, 7 * CHUNK:SEQ]).then_inc(turned_v, 1)
                else:
                    pe.wait_ge(band_ready, 1)
                    pe.wait_ge(cache_in, 32)
                    turn(bS[:, 0:P], k_cache[:])
                    turn(bS[:, P:2 * P], zk[:, SEQ - WINDOW:SEQ])
                    turn(bS[0:DEC, 2 * P:3 * P], zv[:, SEQ:T])
                    turn(bS[0:DEC, 3 * P:4 * P], zk[:, SEQ + WINDOW:SEQ + WINDOW + DEC]).then_inc(turned_v, 1)

            def mix_ready(v):
                tile, h = MIX_UNITS[v]
                if h == A:
                    pe.wait_ge(lo_made, C0["mix"] + MIX.index(tile) + 1)
                if v < 4:
                    pe.wait_ge(y_ready, Y0["down1"] + 2 * KD - 3 + v)
                else:
                    pe.wait_ge(z_ready, v - 3)

            for h in (A, B):
                units = [(U0["mix"] + v, C0["mix"] + v % 4, lambda v=v: mix_ready(v)) for v in range(4 * h, 4 * h + 4)]
                if h == A:
                    first_units(units, 1, A, {4: lambda: all_sums(n0 + 2)})
                else:
                    first_units(units, 1, B, {}, {0: lambda: all_sums(n0 + 3)})
            for v, (tile, h) in list(enumerate(MIX_UNITS))[8:]:
                mix_ready(v)
                product(U0["mix"] + v, x_tiles((C0["mix"] + MIX.index(tile)) % SLOTS, h))
                if v in (8, 9):
                    turn_kv(v - 8)
                d = v - 16
                if d == 0:
                    pe.wait_ge(band_ready, 3)
                if 0 <= d < NTASK:
                    scores(d, 0)
                if 1 <= d <= NTASK:
                    turn_probs(d - 1)
                if 2 <= d < NTASK + 2:
                    weigh(d - 2)
                if 0 <= d < NTASK:
                    scores(d, 1)
                if d == 13:
                    all_sums(SUM0["mix"])
                if d == 18:
                    all_sums(SUM0["mix"] + 1)
                    pe.wait_ge(rows_made, 1)
                    pe.wait_ge(probs_turned, NTASK)
                    turn(bT[0:4 * KA, 0:P], conv_rows[:].rearrange("p s r k -> p (s r k)")).then_inc(conv_turned, 1)

            def out_ready(v):
                if v % 8 < 4:
                    pe.wait_ge(lo_made, C0["out"] + v // 8 * 4 + v % 4 + 1)
                if v < 4:
                    pe.wait_ge(z_ready, len(MIX_UNITS) - 3 + v)
                else:
                    pe.wait_ge(y_ready, Y0["out"] + v - 3)

            n1 = SUM0["out"]
            for v in range(2 * KD):
                i, h, pos = v // 8, v % 8 // 4, v % 4
                if i == 0 and pos == 0:
                    units = [(U0["out"] + w, C0["out"] + w % 4, lambda w=w: out_ready(w)) for w in range(v, v + 4)]
                    hooks = {2: lambda: all_sums(SUM0["mix"] + 2), 5: lambda: all_sums(SUM0["mix"] + 3)} if h == A else {}
                    hi_pass(units[0:2], m_hi, h, lambda k: pe.wait_ge(m_hi_made, 8 * h + k + 1), hooks)
                    hi_pass(units[2:4], m_hi, h, lambda k: None)
                    for n, (u, c, _) in enumerate(units):
                        lo_pass(u, c, m_lo, h, None if n else lambda k: pe.wait_ge(m_ready, 8 * h + k + 1))
                if i:
                    out_ready(v)
                    slot = (C0["out"] + 4 + pos) % SLOTS
                    product(U0["out"] + v, [(slot, k, half(m_hi, k, h), half(m_lo, k, h)) for k in range(KD)],
                            {6: lambda: all_sums(n1)} if v == 12 else None)

            up_stage("up2", 2, {2: lambda: all_sums(n1 + 1), 5: lambda: all_sums(n1 + 2)}, {}, n1 + 3)
            def turn_p(part):
                pe.wait_ge(p_in, 32)
                if part < KP:
                    for i in range(XT - 1):
                        tr = turn(misc[:, 2 + part, i * P:(i + 1) * P], p_tok[:, i, part * P:(part + 1) * P])
                    tr.then_inc(p_turned, 1)
                    return
                pe.wait_ge(p_ready, 1)
                for k in range(KP):
                    tr = turn(misc[:, 2, k * DEC:(k + 1) * DEC], p_tok[0:DEC, XT - 1, k * P:(k + 1) * P], DEC)
                tr.then_inc(p_turned, 1)

            n2 = SUM0["down2"]
            down_stage("down2", "up2", {0: {5: lambda: all_sums(n2), 20: lambda: (turn_p(0), turn_p(1))},
                                        1: {13: lambda: turn_p(2), 17: lambda: all_sums(n2 + 1)}})

            def ple_ready(v):
                g, pos = divmod(v, 4)
                i, h = PLE_UNITS[g]
                if h == A and pos < 2:
                    pe.wait_ge(lo_made, C0["ple"] + 2 * i + pos + 1)
                if v < 4:
                    pe.wait_ge(y_ready, Y0["down2"] + 2 * KD - 3 + v)
                else:
                    pe.wait_ge(g_scaled if pos < 2 else h_made, PAIR0["ple"] + 2 * (g - 1) + pos % 2 + 1)

            for g, (i, h) in enumerate(PLE_UNITS):
                gates = [(U0["ple"] + 4 * g + m, C0["ple"] + 2 * i + m, lambda v=4 * g + m: ple_ready(v)) for m in range(2)]
                if i == 0:
                    hi_pass(gates, x_hi, h, lambda k: pe.wait_ge(x_hi_made, 48 + 8 * h + k + 1),
                            {4: lambda: all_sums(n2 + 2)} if h == A else {2: lambda: all_sums(n2 + 3)})
                    for n, (u, c, _) in enumerate(gates):
                        lo_pass(u, c, x_lo, h, None if n else lambda k: pe.wait_ge(x_ready, 48 + 8 * h + k + 1))
                else:
                    for m, (u, c, ready) in enumerate(gates):
                        ready()
                        product(u, x_tiles(c % SLOTS, h),
                                {3: lambda: all_sums(SUM0["ple"])} if g == 6 and m else None)
                if g == 0:
                    pe.wait_ge(p_ready, KP + 1)
                for m in range(2):
                    v, c = 4 * g + 2 + m, C0["ple"] + 2 * i + m
                    ple_ready(v)
                    product(U0["ple"] + v, [(c % SLOTS, KD + k, pT_hi[:, 2 * k + h, 0:HT], pT_lo[:, 2 * k + h, 0:HT])
                                            for k in range(KP)])

            def turn_out(tt):
                n = P if tt < XT - 1 else DEC
                pe.wait_ge(r_ready, 56 if tt < 2 else 64)
                if tt == 3:
                    pe.wait_ge(o_by_act, 2)
                if tt == 4:
                    pe.wait_ge(o_by_act, 4)
                for k in range(KD):
                    tr = turn(out_banks(tt)[0:n, k // 4, k % 4 * P:(k % 4 + 1) * P], r[:, k, tt * P:tt * P + n])
                tr.then_inc(o_turned, 1)
            pe.wait_ge(h_made, PAIR0["ple"] + 2 * KD)
            turn_out(0)
            all_sums(SUM0["ple"] + 1)
            for tt in range(1, XT):
                turn_out(tt)


_INS = ["x_prompt", "x_sample", "cache_attn_k", "cache_attn_v", "cache_conv", "p_prompt", "p_sample",
        "norm_ffn1_pre", "w_ffn1_gate_up", "w_ffn1_down", "norm_ffn1_post",
        "norm_mix_pre", "w_in", "conv_w", "attn_sinks", "norm_attn_out", "norm_conv_out", "w_out",
        "norm_mix_post", "norm_ffn2_pre", "w_ffn2_gate_up", "w_ffn2_down", "norm_ffn2_post",
        "norm_ple_pre", "w_ple_gate", "w_ple_proj", "norm_ple_post"]


def kernel(**inputs):
    import numpy as np
    import concourse.bacc as bacc
    from concourse.bass_utils import run_bass_kernel_spmd

    nc = bacc.Bacc("TRN2", target_bir_lowering=False, num_devices=1, dynamic_dma_scratch_size=1024)
    arrays, tensors = {}, {}
    for name in _INS:
        a = np.ascontiguousarray(inputs[name])
        arrays[name] = a
        tensors[name] = nc.dram_tensor(name, a.shape, mybir.dt.from_np(a.dtype), kind="ExternalInput").ap()
    k, conv = inputs["cache_attn_k"].shape, inputs["cache_conv"].shape
    outs = [("y_prompt", inputs["x_prompt"].shape), ("y_sample", inputs["x_sample"].shape),
            ("new_k_prompt", k), ("new_v_prompt", k), ("new_conv_prompt", conv),
            ("new_k_sample", k), ("new_v_sample", k), ("new_conv_sample", conv)]
    for name, shape in outs:
        tensors[name] = nc.dram_tensor(name, shape, F32, kind="ExternalOutput").ap()
    encoder_layer(nc, tensors)
    result = run_bass_kernel_spmd(nc, [arrays], core_ids=[0]).results[0]
    return tuple(result[name] for name, _ in outs)
```

```python
from contextlib import ExitStack

import concourse.bass as bass
from concourse import mybir

F32 = mybir.dt.float32
F32R = mybir.dt.float32r
ALU = mybir.AluOpType
ACT = mybir.ActivationFunctionType
AX_X = mybir.AxisListType.X

P = 128
SLOTS = 4
MAXK = 11
A, B = 0, 1


def encoder_layer(nc, t):
    SEQ, D = t["x_prompt"].shape[1:]
    DEC = t["x_sample"].shape[1]
    T = SEQ + DEC
    HT = T // 2
    KD = D // P
    FF = t["w_ffn1_down"].shape[1]
    KF = FF // P
    WINDOW = t["cache_attn_k"].shape[2]
    KP = t["p_prompt"].shape[3] // P
    DA = t["norm_attn_out"].shape[1]
    KA = DA // P
    CHUNK, DH = 64, 64
    SCALE = DH ** -0.5
    EPS = 1e-6
    NCH = SEQ // CHUNK
    TB = SEQ - HT
    XT = SEQ // P + 1
    VE = DA + 2 * P
    assert KF == 2 * MAXK and KD + KP <= MAXK and WINDOW == P and D == 2 * DA and KD == 8 and KA == 4

    MIX = ["k", "v", "q0", "q1", "q2", "q3", "c0", "x0", "c1", "x1", "b0", "b1",
           "c2", "x2", "c3", "x3", "b2", "b3"]
    STAGES = [("up1", 2 * KF, 4 * KF, KD), ("down1", 2 * KD, 2 * KD, MAXK), ("mix", len(MIX), 2 * len(MIX), KD),
              ("out", KD, 2 * KD, KD), ("up2", 2 * KF, 4 * KF, KD), ("down2", 2 * KD, 2 * KD, MAXK),
              ("ple", KD, 4 * KD, KD + KP)]
    C0, U0, stage_of, width_of, loads_of = {}, {}, [], [], []
    chunks = units = 0
    for name, n, un, kt in STAGES:
        C0[name], U0[name] = chunks, units
        chunks, units = chunks + n, units + un
        stage_of += [name] * n
        width_of += [kt] * n
        loads_of += [{"out": 3, "ple": 2}.get(name, 2 if name == "mix" and MIX[j][0] == "q" else 1)
                     for j in range(n)]
    NCHUNK = chunks
    UP_GROUPS, DOWN_GROUPS = KF // 2, KD // 2

    def loaded_value(c):
        return 16 * sum(loads_of[c % SLOTS:c + 1:SLOTS])

    COL, nrows = {}, 0
    for name, n in (("norm_ffn1_pre", KD), ("norm_ffn1_post", KD), ("norm_mix_pre", KD),
                    ("norm_attn_out", KA), ("norm_conv_out", KA), ("conv_w", 3 * KA),
                    ("norm_mix_post", KD), ("norm_ffn2_pre", KD), ("norm_ffn2_post", KD),
                    ("norm_ple_pre", KD), ("norm_ple_post", KD), ("cache_conv", 2 * KA)):
        COL[name] = nrows
        nrows += n

    CHAIN = [(None, "norm_ffn1_pre"), ("norm_ffn1_post", "norm_mix_pre"), ("norm_mix_post", "norm_ffn2_pre"),
             ("norm_ffn2_post", "norm_ple_pre"), ("norm_ple_post", None)]
    SQ0 = {"start": 0, "down1": 16, "mix": 48, "out": 64, "down2": 96, "ple": 128}
    Y0 = {"down1": 0, "out": 2 * KD, "down2": 4 * KD}
    PAIR0 = {"up1": 0, "up2": 2 * KF, "ple": 4 * KF}
    HALF0 = {"down1": 0, "down2": KD}
    SUM0 = {"start": 0, "down1": 2, "mix": 6, "out": 10, "down2": 14, "ple": 18}
    SUMMED = [8, 16, 30, 38, 40, 48, 52, 62, 60, 64, 76, 87, 88, 96, 110, 118, 120, 128, 140, 144]
    PLE_UNITS = [(i, h) for g in (0, 2) for h in (A, B) for i in (g, g + 1)]

    TASKS = [(c, p) for p in range(2) for c in range(NCH)] + [("sample", 0)]
    NTASK = len(TASKS)
    MIX_ATTN0 = 10

    ctx = ExitStack()
    with ctx:
        def sb(name, shape, dt=F32):
            return ctx.enter_context(nc.sbuf_tensor(name, shape, dt))

        def sem(name):
            return ctx.enter_context(nc.semaphore(name))

        def overlay(shapes):
            with ExitStack() as o:
                return [o.enter_context(nc.sbuf_tensor(n, s, d)) for n, s, d in shapes]

        r = sb("r", [P, KD, T])
        x_hi = sb("x_hi", [P, KD, T], F32R)
        y_down, = overlay([("y_down", [P, KD, T], F32)])
        x_lo = sb("x_lo", [P, KD, T], F32R)
        raw = sb("raw", [P, SLOTS, MAXK, P])
        w_hi = sb("w_hi", [P, SLOTS, MAXK, P], F32R)
        w_lo = sb("w_lo", [P, SLOTS, MAXK, P], F32R)
        rpre = sb("rpre", [P, 2, HT])
        ssq = sb("ssq", [P, 2, HT])
        sq = sb("sq", [P, 2, HT])
        tG = sb("tG", [P, 2, HT])
        tU = sb("tU", [P, 2, HT])
        ident = sb("ident", [P, P])
        ones = sb("ones", [P, P])
        gT = sb("gT", [P, nrows])
        eps = sb("eps", [P, 1])
        rms_first = sb("rms_first", [P, 1])
        x_tok, g_rows = overlay([("x_tok", [P, XT, D], F32), ("g_rows", [nrows, P], F32)])
        (m_hi, ac, zq, cv, cinp, zk, zv, v_band, probs, probs_t, k_cache, v_cache, k_new, k_own, v_own,
         conv_rows, conv_new, rmix, ssm, sinks, sink, nsink, mx, nm, se, es, rs, den) = overlay([
             ("m_hi", [P, KD, T], F32R),
             ("ac", [P, KD, T], F32),
             ("zq", [P, KA * T], F32), ("cv", [P, KA, T + 2], F32),
             ("cinp", [P, KA, T + 4], F32),
             ("zk", [P, T + WINDOW], F32),
             ("zv", [P, T], F32), ("v_band", [P, NCH, P], F32),
             ("probs", [P, 2, 2, 3 * CHUNK], F32), ("probs_t", [P, 2, 4, P], F32),
             ("k_cache", [P, P], F32), ("v_cache", [P, P], F32), ("k_new", [P, P], F32),
             ("k_own", [DEC, P], F32), ("v_own", [DEC, P], F32),
             ("conv_rows", [P, 2, 2, KA], F32), ("conv_new", [4 * KA, P], F32),
             ("rmix", [P, 2, HT], F32), ("ssm", [P, 4, HT], F32),
             ("sinks", [P, 8], F32), ("sink", [P, 3, 2], F32), ("nsink", [P, 3, 2], F32),
             ("mx", [P, 2, 2], F32), ("nm", [P, 2, 2], F32), ("se", [P, 2, 2], F32),
             ("es", [P, 2, 2], F32), ("rs", [P, 2, 2], F32), ("den", [P, 2, 2], F32)])
        _, m_lo, y_out = overlay([("pad_m_hi", [P, KD, T], F32), ("m_lo", [P, KD, T], F32R),
                                  ("y_out", [P, KD, T], F32)])
        pT_hi, pT_lo, y_ple, p_tok, out_tok, y_gain, rms_tok, rstd_tok = overlay([
            ("pT_hi", [P, 2 * KP, T], F32R), ("pT_lo", [P, 2 * KP, T], F32R), ("y_ple", [P, KD, T], F32),
            ("p_tok", [P, XT, T], F32), ("out_tok", [P, XT, D], F32), ("y_gain", [P, KD, T], F32),
            ("rms_tok", [P, XT + 1], F32), ("rstd_tok", [P, XT], F32)])
        h_hi = sb("h_hi", [P, KF, T], F32R)
        h_lo = sb("h_lo", [P, KF, T], F32R)

        bank = ctx.enter_context(nc.psum_tensor("bank", [P, 4, 512], F32))
        misc = ctx.enter_context(nc.psum_tensor("misc", [P, 4, 512], F32))
        bO, bS, bT = misc[:, 1, :], misc[:, 2, :], misc[:, 3, :]

        w_loaded = [sem(f"w_loaded{s}") for s in range(SLOTS)]
        hi_made, lo_made, half_used = sem("hi_made"), sem("lo_made"), sem("half_used")
        unit_done = sem("unit_done")
        x_in = [sem(f"x_in{i}") for i in range(XT)]
        g_first_in, g_in, cache_in, sink_in, p_in = sem("g_first_in"), sem("g_in"), sem("cache_in"), sem("sink_in"), sem("p_in")
        consts, turned_g, g_made = sem("consts"), sem("turned_g"), sem("g_made")
        x_turned, r_loaded, r_loaded_act = sem("x_turned"), sem("r_loaded"), sem("r_loaded_act")
        y_scaled, r_ready, x_hi_made, x_ready = sem("y_scaled"), sem("r_ready"), sem("x_hi_made"), sem("x_ready")
        first_squared, squared, summed, sum_done = sem("first_squared"), sem("squared"), sem("summed"), sem("sum_done")
        rooted, inverted = sem("rooted"), sem("inverted")
        g_scaled, gate_act, u_scaled = sem("g_scaled"), sem("gate_act"), sem("u_scaled")
        h_made, h_hi_made = sem("h_made"), sem("h_hi_made")
        h_ready = [sem("h_readyA"), sem("h_readyB")]
        y_ready = sem("y_ready")
        z_ready, z_part, conv_step = sem("z_ready"), sem("z_part"), sem("conv_step")
        rows_made, padded, sinks_made = sem("rows_made"), sem("padded"), sem("sinks_made")
        turned_v, band_ready, conv_turned, conv_out = sem("turned_v"), sem("band_ready"), sem("conv_turned"), sem("conv_out")
        scored, max_made, neg_max, sink_arg = sem("scored"), sem("max_made"), sem("neg_max"), sem("sink_arg")
        exp_made, den_made, den_inv, probs_ready = sem("exp_made"), sem("den_made"), sem("den_inv"), sem("probs_ready")
        turned_p, probs_turned, pv_done, attn_ready = sem("turned_p"), sem("probs_turned"), sem("pv_done"), sem("attn_ready")
        m_scaled, m_hi_made, m_ready = sem("m_scaled"), sem("m_hi_made"), sem("m_ready")
        p_turned, p_hi_made, p_ready = sem("p_turned"), sem("p_hi_made"), sem("p_ready")
        y_gained, r_turned, r_tok_made = sem("y_gained"), sem("r_turned"), sem("r_tok_made")
        y_turned, tok_rooted, tok_inverted, out_made = sem("y_turned"), sem("tok_rooted"), sem("tok_inverted"), sem("out_made")
        stored, state_stored, state_moved = sem("stored"), sem("state_stored"), sem("state_moved")

        MIX_UNITS = [(m, h) for g in range(0, len(MIX), 4) for h in (A, B) for m in MIX[g:g + 4]]

        TASKS_A = NCH + (HT - 1) // CHUNK + 1
        OUT_SQUARES = [("y", A, m) for m in range(4)] + [("y", B, 0), ("y", B, 1)] + [("r", A, k) for k in range(4)] + \
                      [("y", B, 2)] + [("r", A, k) for k in range(4, KD)] + [("y", B, 3)] + [("r", B, k) for k in range(KD)]
        MIX_SQUARES = [(0, k) for k in range(KA)] + [(n, k) for n in (1, 3) for k in (0, 1)] + \
                      [(2, k) for k in range(KA)] + [(n, k) for n in (1, 3) for k in (2, 3)]

        def task_keys(d):
            c = TASKS[d][0]
            return WINDOW + DEC if c == "sample" else min(c + 1, 3) * CHUNK

        def segments(d):
            c = TASKS[d][0]
            if c == "sample":
                return [(0, WINDOW, 0, v_cache[:]), (WINDOW, DEC, 1, v_own[:])]
            if c == 0:
                return [(0, CHUNK, 1, v_band[0:CHUNK, 0])]
            if c == 1:
                return [(0, P, 0, v_band[:, 0])]
            return [(0, P, 0, v_band[:, c - 2]), (P, CHUNK, 1, v_band[0:CHUNK, c])]

        up = {s: t[w][0].rearrange("(k p) (h f c) -> h f p k c", p=P, h=2, c=P)
              for s, w in (("up1", "w_ffn1_gate_up"), ("up2", "w_ffn2_gate_up"))}
        down = {s: t[w][0].rearrange("(j k p) (m c) -> m j p k c", j=2, p=P, c=P)
                for s, w in (("down1", "w_ffn1_down"), ("down2", "w_ffn2_down"))}
        w_in = t["w_in"][0].rearrange("(k p) n -> p k n", p=P)
        w_out, w_gate, w_proj = t["w_out"][0], t["w_ple_gate"][0], t["w_ple_proj"][0]

        def chunk_loads(c):
            s, j, slot = stage_of[c], c - C0[stage_of[c]], raw[:, c % SLOTS]
            cols = slice(j * P, j * P + P)
            if s == "mix":
                kind = MIX[j]
                if kind[0] == "q":
                    n = int(kind[1])
                    return [(slot[:, 0:KD, e * DH:(e + 1) * DH],
                             w_in[:, :, e * DA // 2 + n * DH:e * DA // 2 + (n + 1) * DH]) for e in range(2)]
                at = {"k": DA, "v": DA + P}.get(kind)
                if at is None:
                    at = VE + "bcx".index(kind[0]) * DA + int(kind[1]) * P
                return [(slot[:, 0:KD, :], w_in[:, :, at:at + P])]
            if s == "out":
                return [(slot[e * DH:(e + 1) * DH, 0:KA, :],
                         w_out[e * DA // 2:(e + 1) * DA // 2, cols].rearrange("(k p) n -> p k n", p=DH))
                        for e in range(2)] + \
                       [(slot[:, KA:KD, :], w_out[DA:D, cols].rearrange("(k p) n -> p k n", p=P))]
            return [(slot[:, 0:KD, :], w_gate[:, cols].rearrange("(k p) n -> p k n", p=P)),
                    (slot[:, KD:KD + KP, :], w_proj[:, cols].rearrange("(k p) n -> p k n", p=P))]

        def used(c):
            s, j = stage_of[c], c - C0[stage_of[c]]
            if s[:4] == "down":
                i, m = j // 4, j % 4 // 2
                if j % 2 == 0:
                    return half_used, HALF0[s] + 2 * i + m + 1, 2
                return unit_done, U0[s] + 4 * i + 2 + m + 1, 4
            if s == "ple":
                return unit_done, U0[s] + 4 * PLE_UNITS.index((j // 2, B)) + 2 + j % 2 + 1, 8
            i, pos = divmod(j, 4)
            rest = min(4, len(MIX) - 4 * i) if s == "mix" else 4
            return unit_done, U0[s] + 8 * i + rest + pos + 1, 8

        def psum(n):
            return bank[:, n % 4, 0:HT]

        def half(tile, k, h):
            return tile[:, k, h * HT:(h + 1) * HT]

        def gain(name, k):
            return gT[:, COL[name] + k:COL[name] + k + 1]

        def p_parts(dst, n):
            if n == KP:
                src = misc[:, 2, 0:KP * DEC].rearrange("p (k n) -> p k n", k=KP)
                return [(dst[:].rearrange("p (k h) t -> p h k t", h=2)[:, B, :, TB:HT], src)]
            return [(dst[:, 2 * n, 0:HT], misc[:, 2 + n, 0:HT]), (dst[:, 2 * n + 1, 0:TB], misc[:, 2 + n, HT:SEQ])]

        def token_tile(tt):
            return P if tt < XT - 1 else DEC

        def out_banks(tt):
            return (misc[:, 0:2], misc[:, 2:4], misc[:, 0:2], misc[:, 2:4], bank[:, 0:2])[tt]

        TOKEN_SUMS = [((0, 1), misc[:, 3]), ((2, 3, 4), bank[:, 3])]

        def sum_half(n):
            return n if n < 2 else n % 2 if n >= SUM0["ple"] else (n - 2) // 2 % 2

        def sum_place(n):
            return 2 * (n % 2) if SUM0["mix"] <= n < SUM0["out"] else sum_half(n)

        def sum_bank(n):
            return misc[:, sum_place(n), 0:HT]

        block = ctx.enter_context(nc.Block())

        @block.sync
        def _(sp):
            def load_up(s, i):
                for j in range(4):
                    c = C0[s] + j
                    if isinstance(i, int):
                        if c + 4 * i >= SLOTS:
                            sp.wait_ge(lo_made, c + 4 * i - SLOTS + 1)
                    else:
                        sp.wait_ge(lo_made, i * 4 + (c - SLOTS + 1))
                    sp.dma_start(raw[:, c % SLOTS, 0:KD, :], up[s][j % 2, i * 2 + j // 2])\
                        .then_inc(w_loaded[c % SLOTS], 16)

            def load_down(s, i):
                for j in range(4):
                    c = C0[s] + j
                    sp.wait_ge(lo_made, i * 4 + (c - SLOTS + 1))
                    sp.dma_start(raw[:, c % SLOTS], down[s][i * 2 + j // 2, j % 2])\
                        .then_inc(w_loaded[c % SLOTS], 16)

            def load_short(cs):
                for c in cs:
                    sp.wait_ge(lo_made, c - SLOTS + 1)
                    for dst, src in chunk_loads(c):
                        sp.dma_start(dst, src).then_inc(w_loaded[c % SLOTS], 16)

            def load_gains():
                rows = "a (k p) -> (a k) p"
                for name in ("norm_ffn1_post", "norm_mix_pre", "norm_mix_post", "norm_ffn2_pre", "norm_ffn2_post",
                             "norm_ple_pre", "norm_ple_post"):
                    sp.dma_start(g_rows[COL[name]:COL[name] + KD, :], t[name].rearrange(rows, p=P)).then_inc(g_in, 16)
                for name, n, src in (("norm_conv_out", KA, t["norm_conv_out"].rearrange(rows, p=P)),
                                     ("conv_w", 3 * KA, t["conv_w"].rearrange("a j (k p) -> (a j k) p", p=P)),
                                     ("cache_conv", 2 * KA, t["cache_conv"].rearrange("a b j (k p) -> (a b j k) p", p=P))):
                    sp.dma_start(g_rows[COL[name]:COL[name] + n, :], src).then_inc(g_in, 16)
                at = COL["norm_attn_out"]
                for e in range(2):
                    sp.dma_start(g_rows[at:at + KA, e * DH:(e + 1) * DH],
                                 t["norm_attn_out"][0, e * DA // 2:(e + 1) * DA // 2].rearrange("(k p) -> k p", p=DH))\
                        .then_inc(g_in, 16)
                for name in "kv":
                    sp.dma_start(t[f"new_{name}_sample"][0, 0, 0:WINDOW - DEC], t[f"cache_attn_{name}"][0, 0, DEC:WINDOW])\
                        .then_inc(state_moved, 16)

            for i in range(XT - 1):
                sp.dma_start(x_tok[:, i, :], t["x_prompt"][0, i * P:(i + 1) * P, :]).then_inc(x_in[i], 16)
            sp.dma_start(x_tok[0:DEC, XT - 1, :], t["x_sample"][0]).then_inc(x_in[XT - 1], 16)
            for s, d in (("up1", "down1"), ("up2", "down2")):
                load_up(s, 0)
                if s == "up1":
                    load_gains()
                with sp.Fori(1, UP_GROUPS) as i:
                    load_up(s, i)
                with sp.Fori(0, DOWN_GROUPS) as i:
                    load_down(d, i)
                if s == "up1":
                    mix, flat, rows = C0["mix"], "a b w g d -> (a b w) (g d)", "a b j (k p) -> (a b j k) p"
                    load_short(range(mix, mix + SLOTS))
                    sp.wait_ge(unit_done, U0["mix"])
                    for name, dst in (("k", k_cache), ("v", v_cache)):
                        sp.dma_start(dst[:], t[f"cache_attn_{name}"][0, 0].rearrange("w g d -> w (g d)")).then_inc(cache_in, 16)
                    sp.dma_start(sinks[:], t["attn_sinks"].to_broadcast([P, 8])).then_inc(sink_in, 16)
                    load_short(range(mix + SLOTS, mix + 4 * SLOTS))
                    sp.wait_ge(band_ready, 3)
                    for name, prompt, sample in (("k", k_new[:], k_own[:]), ("v", v_band[:, NCH - 2, :], v_own[:])):
                        sp.dma_start(t[f"new_{name}_prompt"].rearrange(flat), prompt).then_inc(state_stored, 16)
                        sp.dma_start(t[f"new_{name}_sample"].rearrange(flat)[WINDOW - DEC:WINDOW, :], sample)\
                            .then_inc(state_stored, 16)
                    load_short(range(mix + 4 * SLOTS, C0["up2"]))
                    sp.wait_ge(conv_out, 1)
                    for name, at in (("prompt", 0), ("sample", 2 * KA)):
                        sp.dma_start(t[f"new_conv_{name}"].rearrange(rows, p=P), conv_new[at:at + 2 * KA, :])\
                            .then_inc(state_stored, 16)
            load_short(range(C0["ple"], C0["ple"] + SLOTS))
            sp.wait_ge(unit_done, U0["ple"] - 2)
            sp.dma_start(p_tok[:, 0:XT - 1, 0:KP * P], t["p_prompt"][0, 0].rearrange("(i p) n -> p i n", p=P))\
                .then_inc(p_in, 16)
            sp.dma_start(p_tok[0:DEC, XT - 1, 0:KP * P], t["p_sample"][0, 0]).then_inc(p_in, 16)
            load_short(range(C0["ple"] + SLOTS, NCHUNK))
            for tt in range(XT):
                dst = t["y_prompt"][0, tt * P:(tt + 1) * P, :] if tt < XT - 1 else t["y_sample"][0]
                for part in range(2):
                    cols = slice(part * D // 2, (part + 1) * D // 2)
                    sp.wait_ge(out_made, 2 * tt + part + 1)
                    sp.dma_start(dst[:, cols], out_tok[0:token_tile(tt), tt, cols]).then_inc(stored, 16)
            sp.wait_ge(stored, 16 * 2 * XT)
            sp.wait_ge(state_moved, 16 * 2)

        @block.gpsimd
        def _(pool):
            nc.gpsimd.memset(ones[:], 1.0).then_inc(consts, 1)
            nc.gpsimd.memset(eps[:], EPS).then_inc(consts, 1)
            nc.gpsimd.memset(ident[:], 0.0).then_inc(consts, 1)
            pool.wait_ge(consts, 3)
            nc.gpsimd.affine_select(out=ident[:], in_=ident[:], compare_op=ALU.not_equal, fill=1.0, base=0,
                                    pattern=[[-1, P]], channel_multiplier=1).then_inc(consts, 1)

            def add(s, dst, first, i=0, per=0):
                if s < KD:
                    pool.wait_ge(first_squared, s + 1)
                else:
                    pool.wait_ge(squared, i * per + (s + 1 - KD))
                if first:
                    nc.gpsimd.tensor_copy(dst, sq[:, s % 2, :]).then_inc(summed, 1)
                else:
                    pool.wait_ge(summed, i * per + s)
                    nc.gpsimd.tensor_tensor(dst, dst, sq[:, s % 2, :], ALU.add).then_inc(summed, 1)

            def run(s, h, n, fresh):
                for k in range(n):
                    add(s + k, ssq[:, h, :], fresh and k == 0)

            def groups(s0, per_half, n_groups):
                run(s0, A, per_half, True)
                run(s0 + per_half, B, per_half, True)
                if n_groups > 3:
                    with pool.Fori(1, n_groups - 1) as i:
                        for j in range(2 * per_half):
                            add(s0 + j, ssq[:, j // per_half, :], False, i, 2 * per_half)
                last = s0 + 2 * per_half * (n_groups - 1)
                return last

            def last_group(s, per_half):
                for h in (A, B):
                    run(s, h, per_half, False)
                    run(s + per_half, h, KD, True)
                    s += per_half + KD

            run(SQ0["start"], A, KD, True)
            run(SQ0["start"] + KD, B, KD, True)
            last_group(groups(SQ0["down1"], 2, DOWN_GROUPS), 2)
            pool.wait_ge(unit_done, U0["mix"])
            nc.gpsimd.memset(cinp[:, :, 0:2], 0.0).then_inc(padded, 1)
            at = COL["cache_conv"]
            nc.gpsimd.tensor_copy(cinp[:, :, SEQ + 2:SEQ + 4],
                                  gT[:, at:at + 2 * KA].rearrange("p (r k) -> p k r", r=2)).then_inc(padded, 1)
            for j, (n, k) in enumerate(MIX_SQUARES):
                add(SQ0["mix"] + j, ssm[:, n, :], k == 0)
            for h in (A, B):
                run(SQ0["out"] + 4 * h, h, 4, True)
            for j, (kind, h, k) in enumerate(OUT_SQUARES):
                add(SQ0["out"] + 8 + j, ssq[:, h, :], kind == "r" and k == 0)
            last_group(groups(SQ0["down2"], 2, DOWN_GROUPS), 2)
            for g in range(2):
                for h in (A, B):
                    run(SQ0["ple"] + 8 * g + 4 * h, h, 4, g == 0)

        @block.scalar
        def _(act):
            def split_hi(c, i=0):
                n, s = width_of[c], c % SLOTS
                act.wait_ge(w_loaded[s], i * 16 + loaded_value(c))
                if c >= SLOTS:
                    semaphore, value, per = used(c - SLOTS)
                    act.wait_ge(semaphore, i * per + value)
                nc.scalar.activation(w_hi[:, s, 0:n, :], raw[:, s, 0:n, :], ACT.Copy).then_inc(hi_made, 1)

            def square(src, s, i=0, per=0):
                if s >= 2:
                    act.wait_ge(summed, i * per + (s - 1))
                return nc.scalar.activation(sq[:, s % 2, :], src, ACT.Square)

            def root(n, size):
                act.wait_ge(sum_done, n + 1)
                nc.scalar.activation(sum_bank(n), sum_bank(n), ACT.Sqrt, bias=eps[:], scale=1.0 / size)\
                    .then_inc(rooted, 1)

            def high(ci, k, h):
                nc.scalar.activation(half(x_hi, k, h), half(r, k, h), ACT.Copy, scale=gain(CHAIN[ci][1], k))\
                    .then_inc(x_hi_made, 1)

            def chain(ci, h, s, after={}, ks=range(KD)):
                for k in ks:
                    if ci:
                        act.wait_ge(r_ready, 16 * (ci - 1) + 8 * h + k + 1)
                    high(ci, k, h)
                    square(half(r, k, h), s + k).then_inc(squared, 1)
                    if k in after:
                        after[k]()

            def up_gate(s, h, j, i):
                act.wait_ge(g_scaled, i * 4 + (PAIR0[s] + 2 * h + j + 1))
                nc.scalar.activation(tG[:, j, :], tG[:, j, :], ACT.Silu).then_inc(gate_act, 1)

            def up_hi(s, h, j, i):
                p0 = PAIR0[s] + 2 * h + j
                act.wait_ge(h_made, i * 4 + (p0 + 1))
                nc.scalar.activation(half(h_hi, i * 2 + j, h), tU[:, j, :], ACT.Copy).then_inc(h_hi_made, 1)

            def evacuate(u, y_tile, s, i=0):
                act.wait_ge(unit_done, i * 4 + (u + 1))
                square(psum(u), s, i, 4).then_inc(squared, 1)
                nc.scalar.activation(y_tile, psum(u), ACT.Copy).then_inc(y_ready, 1)

            def up_pair(s, h, j, i):
                up_gate(s, h, j, i)
                up_hi(s, h, j, i)

            def second_half(c, step, i=0):
                for j in range(4):
                    split_hi(c + SLOTS + j, i)
                    if j == 1:
                        step(B, 0)
                step(B, 1)

            def group(c, step, i=0):
                step(A, 0), step(A, 1)
                second_half(c, step, i)

            def p_hi(n):
                act.wait_ge(p_turned, n + 1)
                for dst, src in p_parts(pT_hi, n):
                    i = nc.scalar.activation(dst, src, ACT.Copy)
                i.then_inc(p_hi_made, 1)

            def last_group(c, step, ci, s_a, n0, with_p=False):
                step(A, 0), step(A, 1)
                root(n0, D)
                split_hi(c + SLOTS)
                chain(ci, A, s_a, {3: lambda: split_hi(c + SLOTS + 1)})
                if with_p:
                    p_hi(0), p_hi(1)
                step(B, 0)
                split_hi(c + SLOTS + 2)
                if with_p:
                    p_hi(2)
                root(n0 + 1, D)
                step(B, 1)
                split_hi(c + SLOTS + 3)
                root(n0 + 2, D)

            def up_stage(s, ci, s_b, n_pre):
                g0 = C0[s]
                chain(ci, B, s_b, {4: lambda: up_gate(s, A, 0, 0)} if ci else {2: lambda: root(0, D)})
                if not ci:
                    up_gate(s, A, 0, 0)
                up_gate(s, A, 1, 0)
                up_hi(s, A, 0, 0), up_hi(s, A, 1, 0)
                root(n_pre, D)
                second_half(g0, lambda h, j: up_pair(s, h, j, 0))
                with act.Fori(1, UP_GROUPS - 1) as i:
                    group(g0, lambda h, j: up_pair(s, h, j, i), i)
                last = UP_GROUPS - 1
                group(g0 + 4 * last, lambda h, j: up_pair(s, h, j, last))

            def down_stage(s, ci):
                g0, s0, n0, last = C0[s], SQ0[s], SUM0[s], DOWN_GROUPS - 1

                def step(i):
                    return lambda h, j: evacuate(U0[s] + 2 * h + j, half(y_down, i * 2 + j, h), s0 + 2 * h + j, i)
                group(g0, step(0))
                with act.Fori(1, last) as i:
                    group(g0, step(i), i)
                sl = s0 + 4 * last

                def last_step(h, j):
                    evacuate(U0[s] + 4 * last + 2 * h + j, half(y_down, 2 * last + j, h), sl + h * (2 + KD) + j)

                last_group(g0 + 4 * last, last_step, ci, sl + 2, n0, s == "down2")

            act.dma_start(g_rows[0:KD, :], t["norm_ffn1_pre"].rearrange("a (k p) -> (a k) p", p=P)).then_inc(g_first_in, 16)
            act.wait_ge(consts, 4)
            nc.scalar.activation(rms_first[:], eps[:], ACT.Sqrt)
            act.wait_ge(g_made, 1)
            for k in range(KD):
                if k % 2:
                    act.wait_ge(x_turned, k + 1)
                    nc.scalar.activation(r[:, k, 0:SEQ], misc[:, k % 4, :], ACT.Copy).then_inc(r_loaded_act, 1)
                    act.wait_ge(r_loaded, k // 2 + 1)
                    high(0, k - 1, A)
                    act.wait_ge(r_loaded_act, k // 2 + 1)
                    high(0, k, A)
                if k in (4, 6):
                    split_hi(k // 2 - 2)
            split_hi(2), split_hi(3)
            act.wait_ge(r_loaded, KD // 2 + 1)
            up_stage("up1", 0, KD, 1)
            down_stage("down1", 1)

            def mix_first():
                chain(1, B, SQ0["mix"] - KD)
                root(SUM0["down1"] + 3, D)

            def softmax_exp(d):
                b, n = d % 2, task_keys(d)
                act.wait_ge(neg_max, d + 1)
                for g in range(2):
                    nc.scalar.activation(probs[:, b, g, 0:n], bS[:, g * 192:g * 192 + n], ACT.Exp,
                                         bias=nm[:, b, g:g + 1], scale=SCALE, accum_out=rs[:, b, g:g + 1])
                act.wait_ge(sink_arg, d + 1)
                nc.scalar.activation(es[:, b, :], se[:, b, :], ACT.Exp).then_inc(exp_made, 1)

            def copy_probs(d):
                act.wait_ge(turned_p, d + 1)
                segs = segments(d)
                for n, (_, rows, place, _) in enumerate(segs):
                    a = nc.scalar.activation(
                        probs_t[0:rows, d % 2, 2 * place:2 * place + 2, :],
                        bT[0:rows, 2 * place * P:(2 * place + 2) * P].rearrange("p (g q) -> p g q", g=2), ACT.Copy)
                a.then_inc(probs_turned, 1)

            def mix_squares(first, last):
                for j in range(first, last):
                    n, k = MIX_SQUARES[j]
                    h, kind = divmod(n, 2)
                    if kind:
                        act.wait_ge(z_ready, MIX_UNITS.index((f"b{k}", h)) + 1)
                    else:
                        act.wait_ge(attn_ready, TASKS_A if h == A else NTASK)
                    square(half(ac, kind * KA + k, h), SQ0["mix"] + j).then_inc(squared, 1)

            def mix_his(n):
                h, kind = divmod(n, 2)
                for k in range(KA):
                    act.wait_ge(m_scaled, n * KA + k + 1)
                    nc.scalar.activation(half(m_hi, kind * KA + k, h), half(ac, kind * KA + k, h), ACT.Copy,
                                         scale=gain("norm_conv_out" if kind else "norm_attn_out", k))\
                        .then_inc(m_hi_made, 1)

            def mix_root(n):
                root(SUM0["mix"] + n, DA)

            c0 = C0["mix"]
            mix_first()
            for j in range(4):
                split_hi(c0 + SLOTS + j)
            act.wait_ge(turned_v, 1)
            nc.scalar.activation(v_band[:, 0:4, :], bS.rearrange("p (m c) -> p m c", m=4), ACT.Copy).then_inc(band_ready, 1)
            act.wait_ge(turned_v, 2)
            nc.scalar.activation(v_band[:, 4:7, :], bT[:, 0:3 * P].rearrange("p (m c) -> p m c", m=3), ACT.Copy)
            nc.scalar.activation(v_band[0:CHUNK, 7, :], bT[0:CHUNK, 3 * P:4 * P], ACT.Copy).then_inc(band_ready, 1)
            act.wait_ge(turned_v, 3)
            nc.scalar.activation(zk[:, SEQ:SEQ + WINDOW], bS[:, 0:P], ACT.Copy)
            nc.scalar.activation(k_new[:], bS[:, P:2 * P], ACT.Copy)
            nc.scalar.activation(v_own[:], bS[0:DEC, 2 * P:3 * P], ACT.Copy)
            nc.scalar.activation(k_own[:], bS[0:DEC, 3 * P:4 * P], ACT.Copy).then_inc(band_ready, 1)
            for v in range(MIX_ATTN0, len(MIX_UNITS)):
                d = v - MIX_ATTN0
                if 1 <= d <= NTASK:
                    copy_probs(d - 1)
                if d < NTASK:
                    softmax_exp(d)
                if v % 8 >= 4 and v < 32:
                    split_hi(c0 + SLOTS + 4 * (v // 8) + v % 4)
                if v == 25:
                    mix_squares(0, KA)
                if v == 27:
                    mix_squares(KA, 2 * KA)
                if v == 29:
                    mix_squares(2 * KA, 3 * KA)
                if v == 32:
                    mix_root(0)
                    mix_his(0)
                if v == 33:
                    mix_squares(3 * KA, 3 * KA + 2)
                if v == 34:
                    mix_root(1)
                    split_hi(c0 + 20)
                    mix_squares(3 * KA + 2, 3 * KA + 3)
                if v == 35:
                    mix_his(1)
                    mix_squares(3 * KA + 3, 3 * KA + 4)
                    split_hi(c0 + 21)
            act.wait_ge(conv_turned, 1)
            nc.scalar.activation(conv_new[:], bT[0:4 * KA, 0:P], ACT.Copy).then_inc(conv_out, 1)
            mix_root(2)
            mix_his(2)
            mix_root(3)
            mix_his(3)

            def out_evacuate(i, h, m):
                number = SQ0["out"] + (4 * h + m if i == 0 else 8 + OUT_SQUARES.index(("y", h, m)))
                evacuate(U0["out"] + 8 * i + 4 * h + m, half(y_out, 4 * i + m, h), number)

            group(C0["out"], lambda h, j: (out_evacuate(0, h, 2 * j), out_evacuate(0, h, 2 * j + 1)))
            c1, squares = C0["out"] + 2 * SLOTS, SQ0["out"] + 8
            for m in range(4):
                out_evacuate(1, A, m)
            root(SUM0["out"], D)
            out_evacuate(1, B, 0)
            split_hi(c1)
            out_evacuate(1, B, 1)
            split_hi(c1 + 1)
            chain(2, A, squares + OUT_SQUARES.index(("r", A, 0)), ks=range(0, 4))
            out_evacuate(1, B, 2)
            split_hi(c1 + 2)
            chain(2, A, squares + OUT_SQUARES.index(("r", A, 4)) - 4, ks=range(4, KD))
            out_evacuate(1, B, 3)
            split_hi(c1 + 3)
            root(SUM0["out"] + 1, D)
            root(SUM0["out"] + 2, D)

            act.wait_ge(state_stored, 16 * 6)
            up_stage("up2", 2, SQ0["down2"] - KD, SUM0["out"] + 3)
            down_stage("down2", 3)

            def ple_gate(g):
                for m in range(2):
                    act.wait_ge(g_scaled, 4 * KF + 2 * g + m + 1)
                    nc.scalar.activation(tG[:, m, :], tG[:, m, :], ACT.Sigmoid).then_inc(gate_act, 1)

            def ple_square(g):
                i, h = PLE_UNITS[g]
                for m in range(2):
                    act.wait_ge(h_made, 4 * KF + 2 * g + m + 1)
                    y = half(y_ple, 2 * i + m, h)
                    square(y, SQ0["ple"] + 2 * g + m).then_inc(squared, 1)
                    nc.scalar.activation(half(y_gain, 2 * i + m, h), y, ACT.Copy, scale=gain("norm_ple_post", 2 * i + m))\
                        .then_inc(y_gained, 1)

            def copy_r(tt):
                n = token_tile(tt)
                act.wait_ge(r_turned, tt + 1)
                nc.scalar.activation(out_tok[0:n, tt, :].rearrange("p (b c) -> p b c", b=2), misc[0:n, 2:4, :], ACT.Copy)\
                    .then_inc(r_tok_made, 1)

            def token_roots(k):
                act.wait_ge(sum_done, SUM0["ple"] + k + 1)
                tiles, columns = TOKEN_SUMS[k]
                whole = [tt for tt in tiles if tt < XT - 1]
                i = nc.scalar.activation(rms_tok[:, whole[0]:whole[-1] + 1], columns[:, 0:len(whole)], ACT.Sqrt,
                                         bias=eps[:], scale=1.0 / D)
                if XT - 1 in tiles:
                    i = nc.scalar.activation(rms_tok[0:DEC, XT - 1:XT], columns[0:DEC, len(whole):len(whole) + 1],
                                             ACT.Sqrt, bias=eps[0:DEC], scale=1.0 / D)
                i.then_inc(tok_rooted, 1)

            chain(3, B, SQ0["ple"] - KD, {3: lambda: ple_gate(0)})
            ple_square(0)
            ple_gate(1)
            ple_square(1)
            copy_r(0)
            root(SUM0["down2"] + 3, D)
            for g in range(2, 2 * DOWN_GROUPS):
                ple_gate(g)
                if g == 6:
                    token_roots(0)
                if g == 2 * DOWN_GROUPS - 1:
                    nc.scalar.activation(rms_tok[:, XT:XT + 1], eps[:], ACT.Sqrt)
                ple_square(g)
                if g < 4:
                    for m in range(2):
                        split_hi(C0["ple"] + 2 * g + m)
                if g <= XT:
                    copy_r(g - 1)
            token_roots(1)
            act.wait_ge(state_stored, 16 * 6)

        @block.vector
        def _(dve):
            def split_lo(c, i=0):
                n, s = width_of[c], c % SLOTS
                dve.wait_ge(hi_made, i * 4 + (c + 1))
                nc.vector.tensor_tensor(w_lo[:, s, 0:n, :], raw[:, s, 0:n, :], w_hi[:, s, 0:n, :].bitcast(F32),
                                        ALU.subtract).then_inc(lo_made, 1)

            def invert(n, dst):
                dve.wait_ge(rooted, n + 1)
                nc.vector.reciprocal(dst, sum_bank(n)).then_inc(inverted, 1)
                dve.wait_ge(inverted, n + 1)

            def chain_r(ci, h, y, n, after={}):
                post, e0 = CHAIN[ci][0], 16 * (ci - 1) + 8 * h

                def scale(k):
                    nc.vector.tensor_tensor(half(y, k, h), sum_bank(n), half(y, k, h), ALU.mult).then_inc(y_scaled, 1)
                invert(n, sum_bank(n))
                scale(0)
                for k in range(KD):
                    if k + 1 < KD:
                        scale(k + 1)
                    dve.wait_ge(y_scaled, e0 + k + 1)
                    nc.vector.scalar_tensor_tensor(half(r, k, h), half(y, k, h), gain(post, k), half(r, k, h),
                                                   ALU.mult, ALU.add).then_inc(r_ready, 1)
                    if k in after:
                        after[k]()

            def chain_lo(ci, h, ks=range(KD)):
                for k in ks:
                    dve.wait_ge(x_hi_made, 16 * ci + 8 * h + k + 1)
                    nc.vector.scalar_tensor_tensor(half(x_lo, k, h), half(r, k, h), gain(CHAIN[ci][1], k),
                                                   half(x_hi, k, h).bitcast(F32), ALU.mult, ALU.subtract)\
                        .then_inc(x_ready, 1)

            def up_scale(s, h, j, i):
                u = U0[s] + 4 * h + 2 * j
                dve.wait_ge(unit_done, i * 8 + (u + 1))
                nc.vector.tensor_tensor(tG[:, j, :], psum(u), rpre[:, h, :], ALU.mult).then_inc(g_scaled, 1)
                dve.wait_ge(unit_done, i * 8 + (u + 2))
                nc.vector.tensor_tensor(tU[:, j, :], psum(u + 1), rpre[:, h, :], ALU.mult).then_inc(u_scaled, 1)

            def up_hidden(s, h, j, i):
                p0 = PAIR0[s] + 2 * h + j
                dve.wait_ge(gate_act, i * 4 + (p0 + 1))
                dve.wait_ge(u_scaled, i * 4 + (p0 + 1))
                nc.vector.tensor_tensor(tU[:, j, :], tG[:, j, :], tU[:, j, :], ALU.mult).then_inc(h_made, 1)
                dve.wait_ge(h_hi_made, i * 4 + (p0 + 1))
                nc.vector.tensor_tensor(half(h_lo, i * 2 + j, h), tU[:, j, :], half(h_hi, i * 2 + j, h).bitcast(F32),
                                        ALU.subtract).then_inc(h_ready[h], 1)

            def up_pair(s, h, j, i):
                up_scale(s, h, j, i)
                up_hidden(s, h, j, i)

            def second_half(c, step=None, i=0):
                for j in range(4):
                    split_lo(c + SLOTS + j, i)
                    if step and j == 1:
                        step(B, 0)
                if step:
                    step(B, 1)

            def group(c, step, i=0):
                step(A, 0), step(A, 1)
                second_half(c, step, i)

            def up_stage(s, ci, y, n_pre):
                g0, last = C0[s], UP_GROUPS - 1
                if ci:
                    chain_r(ci, B, y, n_pre - 1, {4: lambda: up_scale(s, A, 0, 0)})
                else:
                    up_scale(s, A, 0, 0)
                up_scale(s, A, 1, 0)
                up_hidden(s, A, 0, 0), up_hidden(s, A, 1, 0)
                if ci:
                    chain_lo(ci, B)
                invert(n_pre, rpre[:, B, :])
                second_half(g0, lambda h, j: up_pair(s, h, j, 0))
                if not ci:
                    rest_of_gains()
                with dve.Fori(1, last) as i:
                    group(g0, lambda h, j: up_pair(s, h, j, i), i)
                group(g0 + 4 * last, lambda h, j: up_pair(s, h, j, last))

            def p_lo(n):
                dve.wait_ge(p_hi_made, n + 1)
                for (dst, src), (hi, _) in zip(p_parts(pT_lo, n), p_parts(pT_hi, n)):
                    i = nc.vector.tensor_tensor(dst, src, hi.bitcast(F32), ALU.subtract)
                i.then_inc(p_ready, 1)

            def last_group(c, ci, y, n0, with_p=False):
                def splits():
                    split_lo(c + SLOTS), split_lo(c + SLOTS + 1)
                chain_r(ci, A, y, n0, {3: splits} if ci == 2 else {KD - 1: splits})
                if with_p:
                    p_lo(0), p_lo(1)
                split_lo(c + SLOTS + 2)
                if with_p:
                    p_lo(2)
                if ci != 2:
                    invert(n0 + 1, rpre[:, A, :])
                    chain_lo(ci, A, range(0, KD // 2))
                split_lo(c + SLOTS + 3)
                if ci != 2:
                    chain_lo(ci, A, range(KD // 2, KD))
                else:
                    chain_lo(ci, A)
                    invert(n0 + 1, rpre[:, A, :])

            def down_stage(s, ci):
                g0, last = C0[s], DOWN_GROUPS - 1
                second_half(g0)
                with dve.Fori(1, last) as i:
                    second_half(g0, None, i)
                last_group(g0 + 4 * last, ci, y_down, SUM0[s], s == "down2")

            def rest_of_gains():
                rest = slice(KD, nrows)
                dve.wait_ge(turned_g, 2)
                nc.vector.tensor_copy(gT[:, rest], misc[:, 2, rest]).then_inc(g_made, 1)
                dve.wait_ge(g_made, 2)
                for n in ("norm_ffn1_post", "norm_ffn2_post"):
                    g = gT[:, COL[n]:COL[n] + KD]
                    nc.vector.tensor_scalar(g, g, 0.5, None, ALU.mult).then_inc(g_made, 1)
                dve.wait_ge(g_made, 4)

            def first_square(k):
                if k >= 2:
                    dve.wait_ge(summed, k - 1)
                dve.wait_ge(r_loaded_act if k % 2 else r_loaded, k // 2 + 1)
                nc.vector.tensor_tensor(sq[:, k % 2, :], half(r, k, A), half(r, k, A), ALU.mult)\
                    .then_inc(first_squared, 1)

            dve.wait_ge(turned_g, 1)
            nc.vector.tensor_copy(gT[:, 0:KD], bank[:, 0, 0:KD]).then_inc(g_made, 1)
            for k in range(0, KD, 2):
                dve.wait_ge(x_turned, k + 1)
                nc.vector.tensor_copy(r[:, k, 0:SEQ], misc[:, k % 4, :]).then_inc(r_loaded, 1)
                first_square(k // 2)
            dve.wait_ge(x_turned, KD + 1)
            nc.vector.tensor_copy(r[:, :, SEQ:T], bank[:, 3, 0:KD * DEC].rearrange("p (k n) -> p k n", k=KD))\
                .then_inc(r_loaded, 1)
            first_square(4)
            split_lo(0)
            first_square(5), first_square(6)
            split_lo(1)
            first_square(7)
            split_lo(2)
            chain_lo(0, A, range(0, 4))
            split_lo(3)
            chain_lo(0, A, range(4, KD))
            invert(0, rpre[:, A, :])
            chain_lo(0, B)
            up_stage("up1", 0, None, 1)
            down_stage("down1", 1)

            count = {"part": 0, "conv": 0}

            def evacuate(v):
                (tile, h), u = MIX_UNITS[v], U0["mix"] + v
                kind, j = tile[0], int(tile[1:] or 0)
                dve.wait_ge(unit_done, u + 1)
                ps, scale = psum(u), rpre[:, h, :]
                if kind == "v":
                    nc.vector.tensor_tensor(zv[:, h * HT:(h + 1) * HT], ps, scale, ALU.mult).then_inc(z_ready, 1)
                    return
                if kind == "q":
                    q_prompt = zq[:, 0:KA * SEQ].rearrange("p (c k n) -> p k c n", k=KA, n=CHUNK)[:, j]
                    q_sample = zq[:, KA * SEQ:KA * T].rearrange("p (k n) -> p k n", k=KA)[:, j]
                    whole, rest = divmod(HT, CHUNK)
                    if h == A:
                        pieces = [(0, whole * CHUNK, q_prompt[:, 0:whole, :]),
                                  (whole * CHUNK, HT, q_prompt[:, whole, 0:rest])]
                    else:
                        pieces = [(0, CHUNK - rest, q_prompt[:, whole, rest:CHUNK]),
                                  (CHUNK - rest, TB, q_prompt[:, whole + 1:NCH, :]), (TB, HT, q_sample)]
                    for a, b, dst in pieces:
                        src, by = ps[:, a:b], scale[:, a:b]
                        if len(dst.shape) == 3:
                            src, by = (z.rearrange("p (c n) -> p c n", n=CHUNK) for z in (src, by))
                        i = nc.vector.tensor_tensor(dst, src, by, ALU.mult)
                    i.then_inc(z_ready, 1)
                    return
                ranges = [(0, HT)] if h == A else [(0, TB), (TB, HT)]
                if kind in "xb":
                    tmp = (tG if kind == "x" else tU)[:, count["part"] % 2, :]
                    nc.vector.tensor_tensor(tmp, ps, scale, ALU.mult).then_inc(z_part, 1)
                    count["part"] += 1
                    dve.wait_ge(z_part, count["part"])
                if kind == "x":
                    dve.wait_ge(z_ready, MIX_UNITS.index((f"c{j}", h)) + 1)
                if kind == "b":
                    dve.wait_ge(conv_step, count[f"cv{j}{h}"])
                for n, (a, b) in enumerate(ranges):
                    token = h * HT + a
                    pad = 2 if token < SEQ else 4
                    if kind == "k":
                        at = token if token < SEQ else SEQ + WINDOW
                        i = nc.vector.tensor_tensor(zk[:, at:at + b - a], ps[:, a:b], scale[:, a:b], ALU.mult)
                    if kind == "c":
                        i = nc.vector.tensor_tensor(cinp[:, j, token + pad:token + pad + b - a], ps[:, a:b],
                                                    scale[:, a:b], ALU.mult)
                    if kind == "x":
                        dst = cinp[:, j, token + pad:token + pad + b - a]
                        i = nc.vector.tensor_tensor(dst, dst, tmp[:, a:b], ALU.mult)
                    if kind == "b":
                        src = cv[:, j, token + pad - 2:token + pad - 2 + b - a]
                        i = nc.vector.tensor_tensor(ac[:, KA + j, token:token + b - a], src, tmp[:, a:b], ALU.mult)
                i.then_inc(z_ready, 1)
                if kind == "x":
                    if count["conv"] == 0:
                        dve.wait_ge(padded, 2)
                    dve.wait_ge(z_ready, v + 1)
                    a, n = (0, HT) if h == A else (HT, T + 2 - HT)
                    dst = cv[:, j, a:a + n]
                    for tap in range(3):
                        src, w = cinp[:, j, a + tap:a + tap + n], gain("conv_w", tap * KA + j)
                        if tap == 0:
                            i = nc.vector.tensor_scalar(dst, src, w, None, ALU.mult)
                        else:
                            dve.wait_ge(conv_step, count["conv"])
                            i = nc.vector.scalar_tensor_tensor(dst, src, w, dst, ALU.mult, ALU.add)
                        i.then_inc(conv_step, 1)
                        count["conv"] += 1
                    count[f"cv{j}{h}"] = count["conv"]

            def softmax_max(d):
                b, n, p = d % 2, task_keys(d), 2 if TASKS[d][0] == "sample" else TASKS[d][1]
                dve.wait_ge(scored, 2 * d + 2)
                nc.vector.reduce_max(mx[:, b, :], bS[:, 0:384].rearrange("p (g s) -> p g s", g=2)[:, :, 0:n], AX_X)\
                    .then_inc(max_made, 1)
                dve.wait_ge(max_made, d + 1)
                nc.vector.scalar_tensor_tensor(nm[:, b, :], mx[:, b, :], -SCALE, nsink[:, p, :], ALU.mult, ALU.min)\
                    .then_inc(neg_max, 1)
                dve.wait_ge(neg_max, d + 1)
                nc.vector.tensor_tensor(se[:, b, :], sink[:, p, :], nm[:, b, :], ALU.add).then_inc(sink_arg, 1)

            def softmax_scale(d):
                b, n = d % 2, task_keys(d)
                dve.wait_ge(exp_made, d + 1)
                nc.vector.tensor_tensor(den[:, b, :], rs[:, b, :], es[:, b, :], ALU.add).then_inc(den_made, 1)
                dve.wait_ge(den_made, d + 1)
                nc.vector.reciprocal(den[:, b, :], den[:, b, :]).then_inc(den_inv, 1)
                dve.wait_ge(den_inv, d + 1)
                for g in range(2):
                    i = nc.vector.tensor_scalar(probs[:, b, g, 0:n], probs[:, b, g, 0:n], den[:, b, g:g + 1], None,
                                                ALU.mult)
                i.then_inc(probs_ready, 1)

            def attention_out(d):
                c, p = TASKS[d]
                dve.wait_ge(pv_done, d + 1)
                if c == "sample":
                    dst = ac[:, 0:KA, SEQ:T]
                else:
                    dst = ac[:, 2 * p:2 * p + 2, c * CHUNK:(c + 1) * CHUNK]
                nc.vector.tensor_copy(dst, bO[:, 0:P].rearrange("p (t n) -> p t n", n=dst.shape[2]))\
                    .then_inc(attn_ready, 1)

            def mix_scale(n):
                h, kind = divmod(n, 2)
                invert(SUM0["mix"] + n, rmix[:, kind, :])
                for k in range(KA):
                    src = half(ac, kind * KA + k, h)
                    nc.vector.tensor_tensor(src, src, rmix[:, kind, :], ALU.mult).then_inc(m_scaled, 1)

            def mix_los(n):
                h, kind = divmod(n, 2)
                name = "norm_conv_out" if kind else "norm_attn_out"
                for k in range(KA):
                    dve.wait_ge(m_hi_made, n * KA + k + 1)
                    nc.vector.scalar_tensor_tensor(half(m_lo, kind * KA + k, h), half(ac, kind * KA + k, h), gain(name, k),
                                                   half(m_hi, kind * KA + k, h).bitcast(F32), ALU.mult, ALU.subtract)\
                        .then_inc(m_ready, 1)

            def sinks_by_row():
                dve.wait_ge(sink_in, 16)
                for e in range(2):
                    rows = slice(e * DH, (e + 1) * DH)
                    nc.vector.tensor_copy(sink[rows, 0:2, :],
                                          sinks[rows, :].rearrange("r (g p e) -> r e p g", g=2, p=2)[:, e])\
                        .then_inc(sinks_made, 1)
                for q in range(4):
                    rows = slice(q * DEC, (q + 1) * DEC)
                    nc.vector.tensor_copy(sink[rows, 2, :], sinks[rows, q:8:4]).then_inc(sinks_made, 1)
                dve.wait_ge(sinks_made, 6)
                nc.vector.tensor_scalar(nsink[:], sink[:], -1.0, None, ALU.mult).then_inc(sinks_made, 1)
                dve.wait_ge(sinks_made, 7)

            c0 = C0["mix"]
            chain_r(1, B, y_down, SUM0["down1"] + 2, {4: lambda: (evacuate(0), evacuate(1))})
            for v in range(2, len(MIX_UNITS)):
                d = v - MIX_ATTN0
                evacuate(v)
                if v == 3:
                    chain_lo(1, B)
                    invert(SUM0["down1"] + 3, rpre[:, B, :])
                    sinks_by_row()
                if 0 <= d < NTASK:
                    softmax_max(d)
                if v < 8 and v >= 4:
                    split_lo(c0 + SLOTS + v % 4)
                if v > 8 and (v - 1) % 8 >= 4 and v <= 32:
                    split_lo(c0 + SLOTS + 4 * ((v - 1) // 8) + (v - 1) % 4)
                if v == 32:
                    for s, at in enumerate((SEQ, T + 2)):
                        i = nc.vector.tensor_copy(conv_rows[:, s], cinp[:, :, at:at + 2].rearrange("p k r -> p r k"))
                    i.then_inc(rows_made, 1)
                if 2 <= d < NTASK + 2:
                    attention_out(d - 2)
                if 0 <= d < NTASK:
                    softmax_scale(d)
                if v == 32:
                    mix_scale(0)
                if v == 33:
                    mix_los(0)
                if v == 34:
                    mix_scale(1)
            split_lo(c0 + 20)
            split_lo(c0 + 21)
            mix_los(1)
            mix_scale(2)
            mix_los(2)
            mix_scale(3)
            mix_los(3)

            second_half(C0["out"])
            last_group(C0["out"] + 4, 2, y_out, SUM0["out"])

            up_stage("up2", 2, y_out, SUM0["out"] + 3)
            down_stage("down2", 3)

            def ple_gate(g):
                dve.wait_ge(h_made, PAIR0["ple"] + 2 * g)
                for m in range(2):
                    u = U0["ple"] + 4 * g + m
                    dve.wait_ge(unit_done, u + 1)
                    nc.vector.tensor_tensor(tG[:, m, :], psum(u), rpre[:, PLE_UNITS[g][1], :], ALU.mult)\
                        .then_inc(g_scaled, 1)

            def ple_mul(g):
                i, h = PLE_UNITS[g]
                for m in range(2):
                    u = U0["ple"] + 4 * g + 2 + m
                    dve.wait_ge(gate_act, PAIR0["ple"] + 2 * g + m + 1)
                    dve.wait_ge(unit_done, u + 1)
                    nc.vector.tensor_tensor(half(y_ple, 2 * i + m, h), psum(u), tG[:, m, :], ALU.mult).then_inc(h_made, 1)

            def token_inverse(k):
                dve.wait_ge(tok_rooted, k + 1)
                tiles = TOKEN_SUMS[k][0]
                whole = [tt for tt in tiles if tt < XT - 1]
                cols = slice(whole[0], whole[-1] + 1)
                i = nc.vector.reciprocal(rstd_tok[:, cols], rms_tok[:, cols])
                if XT - 1 in tiles:
                    i = nc.vector.reciprocal(rstd_tok[0:DEC, XT - 1:XT], rms_tok[0:DEC, XT - 1:XT])
                i.then_inc(tok_inverted, 1)
                dve.wait_ge(tok_inverted, k + 1)

            def finish(tt):
                n = token_tile(tt)
                dve.wait_ge(y_turned, tt + 1)
                dve.wait_ge(r_tok_made, tt + 1)
                for part in range(2):
                    out = out_tok[0:n, tt, part * D // 2:(part + 1) * D // 2]
                    nc.vector.scalar_tensor_tensor(out, out_banks(tt)[0:n, part, :], rstd_tok[0:n, tt:tt + 1], out,
                                                   ALU.mult, ALU.add).then_inc(out_made, 1)

            chain_r(3, B, y_down, SUM0["down2"] + 2, {3: lambda: ple_gate(0)})
            ple_mul(0)
            ple_gate(1)
            chain_lo(3, B)
            ple_mul(1)
            invert(SUM0["down2"] + 3, rpre[:, B, :])
            for g in range(2, 2 * DOWN_GROUPS):
                ple_gate(g)
                ple_mul(g)
                if g < 4:
                    for m in range(2):
                        split_lo(C0["ple"] + 2 * g + m)
                if g == 6:
                    token_inverse(0)
                    finish(0), finish(1)
            token_inverse(1)
            for tt in range(2, XT):
                finish(tt)

        @block.tensor
        def _(pe):
            def product(u, tiles, hooks=None, marks=None):
                n = len(tiles)
                for k, (slot, kk, hi, lo) in enumerate(tiles):
                    if hooks and k in hooks:
                        hooks[k]()
                    wh, wl = w_hi[:, slot, kk, :], w_lo[:, slot, kk, :]
                    nc.tensor.matmul(psum(u), wh, hi, start=(k == 0), stop=False)
                    nc.tensor.matmul(psum(u), wh, lo, start=False, stop=False)
                    mm = nc.tensor.matmul(psum(u), wl, hi, start=False, stop=(k == n - 1))
                    if marks and k in marks:
                        mm.then_inc(marks[k], 1)
                mm.then_inc(unit_done, 1)

            def all_sums(n, size=None):
                pe.wait_ge(summed, SUMMED[n])
                last = [m for m in range(n) if sum_place(m) == sum_place(n)]
                if last:
                    pe.wait_ge(inverted, last[-1] + 1)
                k = n - SUM0["mix"]
                if k == 1:
                    pe.wait_ge(exp_made, NTASK)
                src = ssm[:, k, :] if 0 <= k < 4 else ssq[:, sum_half(n), :]
                nc.tensor.matmul(sum_bank(n), ones[:], src, start=True, stop=True).then_inc(sum_done, 1)

            def hi_pass(pair, x_hi, h, wait, hooks={}):
                for k in range(KD):
                    wait(k)
                    if k in hooks:
                        hooks[k]()
                    for u, c, ready in pair:
                        if k == 0:
                            ready()
                        for w in (w_hi, w_lo):
                            nc.tensor.matmul(psum(u), w[:, c % SLOTS, k, :], half(x_hi, k, h),
                                             start=(k == 0 and w is w_hi), stop=False)

            def lo_pass(u, c, x_lo, h, wait=None):
                for k in range(KD):
                    if wait:
                        wait(k)
                    mm = nc.tensor.matmul(psum(u), w_hi[:, c % SLOTS, k, :], half(x_lo, k, h),
                                          start=False, stop=(k == KD - 1))
                mm.then_inc(unit_done, 1)

            def first_units(units, ci, h, hooks_hi={}, hooks_lo={}, second={}):
                hi_pass(units[0:2], x_hi, h, lambda k: pe.wait_ge(x_hi_made, 16 * ci + 8 * h + k + 1), hooks_hi)
                if units[2:4]:
                    hi_pass(units[2:4], x_hi, h, lambda k: None, second)
                for n, (u, c, _) in enumerate(units):
                    lo_pass(u, c, x_lo, h, None if n else lambda k: pe.wait_ge(x_ready, 16 * ci + 8 * h + k + 1))
                    if n in hooks_lo:
                        hooks_lo[n]()

            def x_tiles(slot, h):
                return [(slot, k, half(x_hi, k, h), half(x_lo, k, h)) for k in range(KD)]

            def up_ready(s, i, h, pos):
                if h == A:
                    pe.wait_ge(lo_made, i * 4 + (C0[s] + pos + 1))
                if s == "up1" and isinstance(i, int) and h == A and pos in (0, 3):
                    pe.wait_ge(g_made if pos == 0 else r_loaded, 1 if pos == 0 else KD // 2 + 1)
                if not (isinstance(i, int) and i == 0 and h == A):
                    pe.wait_ge(g_scaled if pos % 2 == 0 else u_scaled, i * 4 + (PAIR0[s] + 2 * h + pos // 2 - 2 + 1))
                elif s == "up2":
                    pe.wait_ge(y_ready, Y0["out"] + 2 * KD - 3 + pos)

            def up_stage(s, ci, hooks_hi, second, n_pre, after_b=lambda: None):
                for h in (A, B):
                    units = [(U0[s] + 4 * h + pos, C0[s] + pos, lambda h=h, pos=pos: up_ready(s, 0, h, pos))
                             for pos in range(4)]
                    if h == A:
                        first_units(units, ci, A, hooks_hi, {}, second)
                    else:
                        first_units(units, ci, B, {}, {0: after_b}, {4: lambda: all_sums(n_pre)})
                with pe.Fori(1, UP_GROUPS) as i:
                    for h in (A, B):
                        for pos in range(4):
                            up_ready(s, i, h, pos)
                            product(U0[s] + 4 * h + pos, x_tiles((C0[s] + pos) % SLOTS, h))

            def down_group(s, i, up_s, hooks_b={}):
                for h in (A, B):
                    if isinstance(i, int) and i == 0:
                        pe.wait_ge(h_ready[h], KF * (1 if s == "down1" else 2))
                    for m in range(2):
                        u, c = U0[s] + 2 * h + m, C0[s] + 2 * m
                        if h == A:
                            pe.wait_ge(lo_made, i * 4 + (c + 2))
                        if isinstance(i, int) and i == 0:
                            pair = 2 * KF - 2 + h
                            emptied, p0 = (g_scaled, PAIR0[up_s]) if m == 0 else (u_scaled, PAIR0[up_s])
                            pe.wait_ge(emptied, p0 + pair + 1)
                        else:
                            pe.wait_ge(y_ready, i * 4 + (Y0[s] + 2 * h + m - 3))
                        tiles = [((c + k // MAXK) % SLOTS, k % MAXK, half(h_hi, k, h), half(h_lo, k, h))
                                 for k in range(KF)]
                        marks = {MAXK - 1: half_used} if h == B else {}
                        product(u, tiles, hooks_b.get(m) if h == B else None, marks)

            def down_stage(s, up_s, hooks_b):
                last = DOWN_GROUPS - 1
                down_group(s, 0, up_s)
                with pe.Fori(1, last) as i:
                    down_group(s, i, up_s)
                down_group(s, last, up_s, hooks_b)

            def turn(dst, src, n=P):
                return nc.tensor.transpose(dst, src, ident[0:n, 0:n])

            pe.wait_ge(consts, 4)
            pe.wait_ge(g_first_in, 16)
            turn(bank[:, 0, 0:KD], g_rows[0:KD, :], KD).then_inc(turned_g, 1)
            for k in range(KD):
                if k >= 4:
                    pe.wait_ge(r_loaded_act if k % 2 else r_loaded, (k - 4) // 2 + 1)
                for i in range(XT - 1):
                    if k == 0:
                        pe.wait_ge(x_in[i], 16)
                    tr = turn(misc[:, k % 4, i * P:(i + 1) * P], x_tok[:, i, k * P:(k + 1) * P])
                tr.then_inc(x_turned, 1)
            pe.wait_ge(x_in[XT - 1], 16)
            for k in range(KD):
                tr = turn(bank[:, 3, k * DEC:(k + 1) * DEC], x_tok[0:DEC, XT - 1, k * P:(k + 1) * P], DEC)
            tr.then_inc(x_turned, 1)

            def turn_gains():
                pe.wait_ge(g_in, 16 * 12)
                turn(misc[:, 2, 0:nrows], g_rows[:], nrows).then_inc(turned_g, 1)

            up_stage("up1", 0, {}, {2: lambda: all_sums(0)}, 1, turn_gains)
            n0 = SUM0["down1"]
            down_stage("down1", "up1", {0: {5: lambda: all_sums(n0)}, 1: {17: lambda: all_sums(n0 + 1)}})

            def scores(d, g):
                c, p = TASKS[d]
                if g:
                    pe.wait_ge(scored, 2 * d + 1)
                elif d:
                    pe.wait_ge(exp_made, d)
                rows = slice(g * DH, (g + 1) * DH)
                if c == "sample":
                    q, keys = zq[rows, KA * SEQ:KA * T], zk[rows, SEQ:SEQ + WINDOW + DEC]
                else:
                    q = zq[rows, (2 * c + p) * P:(2 * c + p + 1) * P]
                    keys = zk[rows, max(c - 2, 0) * CHUNK:(c + 1) * CHUNK]
                mm = nc.tensor.matmul(bS[:, g * 192:g * 192 + task_keys(d)], q, keys, start=True, stop=True)
                mm.then_inc(scored, 1)

            def turn_probs(d):
                pe.wait_ge(probs_ready, d + 1)
                if d:
                    pe.wait_ge(probs_turned, d)
                for first, rows, place, _ in segments(d):
                    for g in range(2):
                        at = (2 * place + g) * P
                        tr = turn(bT[0:rows, at:at + P], probs[:, d % 2, g, first:first + rows])
                tr.then_inc(turned_p, 1)

            def weigh(d):
                pe.wait_ge(probs_turned, d + 1)
                if d:
                    pe.wait_ge(attn_ready, d)
                segs = segments(d)
                for g in range(2):
                    for n, (_, rows, place, values) in enumerate(segs):
                        mm = nc.tensor.matmul(bO[g * DH:(g + 1) * DH, 0:P], values[:, g * DH:(g + 1) * DH],
                                              probs_t[0:rows, d % 2, 2 * place + g, :],
                                              start=(n == 0), stop=(n == len(segs) - 1))
                mm.then_inc(pv_done, 1)

            def turn_kv(part):
                if part == 0:
                    pe.wait_ge(z_ready, 8)
                    for m in range(4):
                        tr = turn(bS[:, m * P:(m + 1) * P], zv[:, m * CHUNK:m * CHUNK + P])
                    tr.then_inc(turned_v, 1)
                    for m in range(4, 7):
                        tr = turn(bT[:, (m - 4) * P:(m - 3) * P], zv[:, m * CHUNK:m * CHUNK + P])
                    turn(bT[0:CHUNK, 3 * P:4 * P], zv[:, 7 * CHUNK:SEQ]).then_inc(turned_v, 1)
                else:
                    pe.wait_ge(band_ready, 1)
                    pe.wait_ge(cache_in, 32)
                    turn(bS[:, 0:P], k_cache[:])
                    turn(bS[:, P:2 * P], zk[:, SEQ - WINDOW:SEQ])
                    turn(bS[0:DEC, 2 * P:3 * P], zv[:, SEQ:T])
                    turn(bS[0:DEC, 3 * P:4 * P], zk[:, SEQ + WINDOW:SEQ + WINDOW + DEC]).then_inc(turned_v, 1)

            def mix_ready(v):
                tile, h = MIX_UNITS[v]
                if h == A:
                    pe.wait_ge(lo_made, C0["mix"] + MIX.index(tile) + 1)
                if v < 4:
                    pe.wait_ge(y_ready, Y0["down1"] + 2 * KD - 3 + v)
                else:
                    pe.wait_ge(z_ready, v - 3)

            for h in (A, B):
                units = [(U0["mix"] + v, C0["mix"] + v % 4, lambda v=v: mix_ready(v)) for v in range(4 * h, 4 * h + 4)]
                if h == A:
                    first_units(units, 1, A, {4: lambda: all_sums(n0 + 2)})
                else:
                    first_units(units, 1, B, {}, {}, {4: lambda: all_sums(n0 + 3)})
            for v, (tile, h) in list(enumerate(MIX_UNITS))[8:]:
                mix_ready(v)
                product(U0["mix"] + v, x_tiles((C0["mix"] + MIX.index(tile)) % SLOTS, h))
                if v in (8, 9):
                    turn_kv(v - 8)
                d = v - MIX_ATTN0
                if d == 0:
                    pe.wait_ge(band_ready, 3)
                if 0 <= d < NTASK:
                    scores(d, 0)
                if 1 <= d <= NTASK:
                    turn_probs(d - 1)
                if 2 <= d < NTASK + 2:
                    weigh(d - 2)
                if 0 <= d < NTASK:
                    scores(d, 1)
                if v in (30, 34, 35):
                    all_sums(SUM0["mix"] + (30, 34, 35).index(v))
                if v == 33:
                    pe.wait_ge(rows_made, 1)
                    pe.wait_ge(probs_turned, NTASK)
                    turn(bT[0:4 * KA, 0:P], conv_rows[:].rearrange("p s r k -> p (s r k)")).then_inc(conv_turned, 1)

            def out_ready(v):
                if v % 8 < 4:
                    pe.wait_ge(lo_made, C0["out"] + v // 8 * 4 + v % 4 + 1)
                if v < 4:
                    pe.wait_ge(z_ready, len(MIX_UNITS) - 3 + v)
                else:
                    pe.wait_ge(y_ready, Y0["out"] + v - 3)

            n1 = SUM0["out"]
            for v in range(2 * KD):
                i, h, pos = v // 8, v % 8 // 4, v % 4
                if i == 0 and pos == 0:
                    units = [(U0["out"] + w, C0["out"] + w % 4, lambda w=w: out_ready(w)) for w in range(v, v + 4)]
                    hooks = {6: lambda: all_sums(SUM0["mix"] + 3)} if h == A else {}
                    hi_pass(units[0:2], m_hi, h, lambda k: pe.wait_ge(m_hi_made, 8 * h + k + 1), hooks)
                    hi_pass(units[2:4], m_hi, h, lambda k: None)
                    for n, (u, c, _) in enumerate(units):
                        lo_pass(u, c, m_lo, h, None if n else lambda k: pe.wait_ge(
                            m_ready, 8 * h + k + 1))
                if i:
                    out_ready(v)
                    slot = (C0["out"] + 4 + pos) % SLOTS
                    product(U0["out"] + v, [(slot, k, half(m_hi, k, h), half(m_lo, k, h)) for k in range(KD)],
                            {6: lambda: all_sums(n1)} if v == 12 else None)

            up_stage("up2", 2, {}, {0: lambda: all_sums(n1 + 1), 2: lambda: all_sums(n1 + 2)}, n1 + 3)
            def turn_p(part):
                pe.wait_ge(p_in, 32)
                if part < KP:
                    for i in range(XT - 1):
                        tr = turn(misc[:, 2 + part, i * P:(i + 1) * P], p_tok[:, i, part * P:(part + 1) * P])
                    tr.then_inc(p_turned, 1)
                    return
                pe.wait_ge(p_ready, 1)
                for k in range(KP):
                    tr = turn(misc[:, 2, k * DEC:(k + 1) * DEC], p_tok[0:DEC, XT - 1, k * P:(k + 1) * P], DEC)
                tr.then_inc(p_turned, 1)

            n2 = SUM0["down2"]
            down_stage("down2", "up2", {0: {5: lambda: all_sums(n2), 20: lambda: (turn_p(0), turn_p(1))},
                                        1: {13: lambda: turn_p(2), 17: lambda: all_sums(n2 + 1)}})

            def ple_ready(v):
                g, pos = divmod(v, 4)
                i, h = PLE_UNITS[g]
                if h == A and pos < 2:
                    pe.wait_ge(lo_made, C0["ple"] + 2 * i + pos + 1)
                if v < 4:
                    pe.wait_ge(y_ready, Y0["down2"] + 2 * KD - 3 + v)
                else:
                    pe.wait_ge(g_scaled if pos < 2 else h_made, PAIR0["ple"] + 2 * (g - 1) + pos % 2 + 1)

            def turn_r(tt):
                n = token_tile(tt)
                if tt == 0:
                    pe.wait_ge(p_ready, KP + 1)
                else:
                    pe.wait_ge(r_tok_made, tt)
                pe.wait_ge(r_ready, 16 * 3)
                for k in range(KD):
                    tr = turn(misc[0:n, 2 + k // 4, k % 4 * P:(k % 4 + 1) * P], r[:, k, tt * P:tt * P + n])
                tr.then_inc(r_turned, 1)

            def turn_y(tt, ks):
                n, last = token_tile(tt), ks[-1] == KD - 1
                if ks[0] == 0:
                    if tt == 1:
                        pe.wait_ge(r_tok_made, XT)
                        pe.wait_ge(tok_rooted, 1)
                    if tt in (2, 3):
                        pe.wait_ge(out_made, 2 * (tt - 1))
                    if tt == 4:
                        pe.wait_ge(g_scaled, PAIR0["ple"] + 2 * 2 * DOWN_GROUPS)
                pe.wait_ge(y_gained, 12 if tt < 2 else 16 if last else 14)
                for k in ks:
                    tr = turn(out_banks(tt)[0:n, k // 4, k % 4 * P:(k % 4 + 1) * P], y_gain[:, k, tt * P:tt * P + n])
                if last:
                    tr.then_inc(y_turned, 1)

            def token_sums(k):
                pe.wait_ge(summed, SUMMED[SUM0["ple"] + k])
                if k == 0:
                    pe.wait_ge(r_tok_made, XT)
                else:
                    pe.wait_ge(h_made, PAIR0["ple"] + 2 * 2 * DOWN_GROUPS)
                tiles, columns = TOKEN_SUMS[k]
                for c, tt in enumerate(tiles):
                    n = token_tile(tt)
                    mm = nc.tensor.matmul(columns[0:n, c:c + 1], ssq[:].rearrange("p h t -> p (h t)")[:, tt * P:tt * P + n],
                                          ones[:, 0:1], start=True, stop=True)
                mm.then_inc(sum_done, 1)

            for g, (i, h) in enumerate(PLE_UNITS):
                gates = [(U0["ple"] + 4 * g + m, C0["ple"] + 2 * i + m, lambda v=4 * g + m: ple_ready(v)) for m in range(2)]
                if i == 0:
                    hi_pass(gates, x_hi, h, lambda k: pe.wait_ge(x_hi_made, 48 + 8 * h + k + 1),
                            {4: lambda: all_sums(n2 + 2)} if h == A else {2: lambda: all_sums(n2 + 3)})
                    for n, (u, c, _) in enumerate(gates):
                        lo_pass(u, c, x_lo, h, None if n else lambda k: pe.wait_ge(x_ready, 48 + 8 * h + k + 1))
                else:
                    for m, (u, c, ready) in enumerate(gates):
                        ready()
                        product(u, x_tiles(c % SLOTS, h),
                                {6: lambda: token_sums(0)} if g == 6 and m else None)
                if g == 0:
                    pe.wait_ge(p_ready, KP + 1)
                if 1 <= g <= XT:
                    turn_r(g - 1)
                if g == 6:
                    turn_y(0, range(KD)), turn_y(1, range(KD))
                if g == 7:
                    turn_y(2, range(KD - 2)), turn_y(3, range(KD - 2))
                for m in range(2):
                    v, c = 4 * g + 2 + m, C0["ple"] + 2 * i + m
                    ple_ready(v)
                    product(U0["ple"] + v, [(c % SLOTS, KD + k, pT_hi[:, 2 * k + h, 0:HT], pT_lo[:, 2 * k + h, 0:HT])
                                            for k in range(KP)])
            turn_y(4, range(KD - 2))
            for tt in range(2, XT):
                turn_y(tt, range(KD - 2, KD))
            token_sums(1)


_INS = ["x_prompt", "x_sample", "cache_attn_k", "cache_attn_v", "cache_conv", "p_prompt", "p_sample",
        "norm_ffn1_pre", "w_ffn1_gate_up", "w_ffn1_down", "norm_ffn1_post",
        "norm_mix_pre", "w_in", "conv_w", "attn_sinks", "norm_attn_out", "norm_conv_out", "w_out",
        "norm_mix_post", "norm_ffn2_pre", "w_ffn2_gate_up", "w_ffn2_down", "norm_ffn2_post",
        "norm_ple_pre", "w_ple_gate", "w_ple_proj", "norm_ple_post"]


def kernel(**inputs):
    import numpy as np
    import concourse.bacc as bacc
    from concourse.bass_utils import run_bass_kernel_spmd

    nc = bacc.Bacc("TRN2", target_bir_lowering=False, num_devices=1, dynamic_dma_scratch_size=1024)
    arrays, tensors = {}, {}
    for name in _INS:
        a = np.ascontiguousarray(inputs[name])
        arrays[name] = a
        tensors[name] = nc.dram_tensor(name, a.shape, mybir.dt.from_np(a.dtype), kind="ExternalInput").ap()
    k, conv = inputs["cache_attn_k"].shape, inputs["cache_conv"].shape
    outs = [("y_prompt", inputs["x_prompt"].shape), ("y_sample", inputs["x_sample"].shape),
            ("new_k_prompt", k), ("new_v_prompt", k), ("new_conv_prompt", conv),
            ("new_k_sample", k), ("new_v_sample", k), ("new_conv_sample", conv)]
    for name, shape in outs:
        tensors[name] = nc.dram_tensor(name, shape, F32, kind="ExternalOutput").ap()
    encoder_layer(nc, tensors)
    result = run_bass_kernel_spmd(nc, [arrays], core_ids=[0]).results[0]
    return tuple(result[name] for name, _ in outs)
```
